# Optimizing a Trainium2 kernel written in Bass

```python
import math
import jax, jax.numpy as jnp
from jax import lax
import numpy as np

D_MODEL = 1024
BATCH = 1
SEQ = 256
DEPTH = 2

MIX_WIDTH = D_MODEL
POOL_WIDTH = MIX_WIDTH // 2
POOL_WINDOWS = (2, 4, 8, 16)
POOL_GROUPS = len(POOL_WINDOWS)
POOL_GC = POOL_WIDTH // POOL_GROUPS
N_HEADS = 4
QK_NOPE = 128
QK_ROPE = 64
V_HEAD = 128
QK_HEAD = QK_NOPE + QK_ROPE
MLA_WIDTH = N_HEADS * V_HEAD
Q_LORA = 384
KV_LORA = 256
ROPE_THETA = 10000.0
SOFTMAX_SCALE = 1.0 / math.sqrt(QK_HEAD)
Q_BLOCK = 128
IN_COLS = POOL_WIDTH + Q_LORA + KV_LORA + QK_ROPE
D_FF = 2816
N_SUBLAYERS = 3
EPS = 1e-6


def rms_norm(x, g):
    xf = x.astype(jnp.float32)
    y = xf * lax.rsqrt(jnp.mean(xf * xf, axis=-1, keepdims=True) + EPS)
    return (y * g.astype(jnp.float32)).astype(x.dtype)

def modulate(h, shift, scale):
    return h * (1 + scale[:, None, :]) + shift[:, None, :]

def swiglu(h, w_gate, w_up, w_down):
    return (jax.nn.silu(h @ w_gate) * (h @ w_up)) @ w_down

def rotate_half(x):
    x1, x2 = jnp.split(x, 2, axis=-1)
    return jnp.concatenate([-x2, x1], axis=-1)

def apply_rope(x, cos, sin):
    return x * cos + rotate_half(x) * sin

def causal_multiscale_pool(u, pool_w, pool_scale):
    B, S, C = u.shape
    cs = jnp.cumsum(u.astype(jnp.float32), axis=1)
    pos = jnp.arange(S)
    means = []
    for g, w in enumerate(POOL_WINDOWS):
        csg = cs[..., g * POOL_GC:(g + 1) * POOL_GC]
        lag = jnp.pad(csg, ((0, 0), (w, 0), (0, 0)))[:, :S]
        cnt = jnp.minimum(pos + 1, w).astype(jnp.float32)[None, :, None]
        means.append((csg - lag) / cnt)
    pooled = jnp.stack(means, axis=2).astype(u.dtype)
    diff = pooled - u.reshape(B, S, POOL_GROUPS, POOL_GC)
    y = jnp.einsum('bsgc,gcd->bsgd', diff, pool_w).reshape(B, S, C)
    return y * pool_scale

def mla_attention(cq, ckv, kr, q_a_norm, w_q_b, kv_a_norm, w_kv_b, cos, sin):
    B, S, _ = cq.shape
    q = (rms_norm(cq, q_a_norm) @ w_q_b).reshape(B, S, N_HEADS, QK_HEAD)
    q_nope, q_rope = q[..., :QK_NOPE], q[..., QK_NOPE:]
    q_rope = apply_rope(q_rope, cos[:, :, None, :], sin[:, :, None, :])
    kv = (rms_norm(ckv, kv_a_norm) @ w_kv_b).reshape(B, S, N_HEADS, QK_NOPE + V_HEAD)
    k_nope, v = kv[..., :QK_NOPE], kv[..., QK_NOPE:]
    k_rope = apply_rope(kr, cos, sin)

    nb = S // Q_BLOCK
    qn = q_nope.reshape(B, nb, Q_BLOCK, N_HEADS, QK_NOPE).transpose(1, 0, 3, 2, 4)
    qr = q_rope.reshape(B, nb, Q_BLOCK, N_HEADS, QK_ROPE).transpose(1, 0, 3, 2, 4)
    kn = k_nope.transpose(0, 2, 1, 3)
    vv = v.transpose(0, 2, 1, 3)
    kpos = jnp.arange(S)

    def block(args):
        qn_b, qr_b, i = args
        s = (jnp.einsum('bhqd,bhkd->bhqk', qn_b, kn)
             + jnp.einsum('bhqd,bkd->bhqk', qr_b, k_rope)).astype(jnp.float32) * SOFTMAX_SCALE
        qpos = i * Q_BLOCK + jnp.arange(Q_BLOCK)
        s = jnp.where(qpos[:, None] >= kpos[None, :], s, -jnp.inf)
        p = jax.nn.softmax(s, axis=-1).astype(vv.dtype)
        return jnp.einsum('bhqk,bhkd->bhqd', p, vv)

    o = lax.map(block, (qn, qr, jnp.arange(nb)))
    return o.transpose(1, 0, 3, 2, 4).reshape(B, S, MLA_WIDTH)

def first_inputs(seed: int = 0) -> dict:
    key = jax.random.key(seed)
    ks = jax.random.split(key, 24)
    f32 = jnp.float32
    nrm = lambda k, shape, s: (jax.random.normal(k, shape, f32) * s)
    gain = lambda k, shape: 1.0 + 0.05 * jax.random.normal(k, shape, f32)
    D, F, L = D_MODEL, D_FF, DEPTH
    x = jax.random.normal(ks[0], (BATCH, SEQ, D), f32)
    c = jax.random.normal(ks[1], (BATCH, D), f32)
    positions = jnp.broadcast_to(jnp.arange(SEQ, dtype=jnp.int32)[None, :], (BATCH, SEQ))
    return {
        "x": x,
        "c": c,
        "positions": positions,
        "ada_w": nrm(ks[2], (L, D, 3 * N_SUBLAYERS * D), 0.5 * D ** -0.5),
        "ada_b": nrm(ks[3], (L, 3 * N_SUBLAYERS * D), 0.01),
        "ffn1_norm": gain(ks[4], (L, D)),
        "ffn1_w_gate": nrm(ks[5], (L, D, F), D ** -0.5),
        "ffn1_w_up": nrm(ks[6], (L, D, F), D ** -0.5),
        "ffn1_w_down": nrm(ks[7], (L, F, D), F ** -0.5),
        "mix_norm": gain(ks[8], (L, D)),
        "w_in": nrm(ks[9], (L, D, IN_COLS), D ** -0.5),
        "pool_w": nrm(ks[10], (L, POOL_GROUPS, POOL_GC, POOL_GC), POOL_GC ** -0.5),
        "pool_scale": gain(ks[11], (L, POOL_WIDTH)),
        "q_a_norm": gain(ks[12], (L, Q_LORA)),
        "w_q_b": nrm(ks[13], (L, Q_LORA, N_HEADS * QK_HEAD), Q_LORA ** -0.5),
        "kv_a_norm": gain(ks[14], (L, KV_LORA)),
        "w_kv_b": nrm(ks[15], (L, KV_LORA, N_HEADS * (QK_NOPE + V_HEAD)), KV_LORA ** -0.5),
        "w_out": nrm(ks[16], (L, MIX_WIDTH, D), MIX_WIDTH ** -0.5),
        "ffn2_norm": gain(ks[17], (L, D)),
        "ffn2_w_gate": nrm(ks[18], (L, D, F), D ** -0.5),
        "ffn2_w_up": nrm(ks[19], (L, D, F), D ** -0.5),
        "ffn2_w_down": nrm(ks[20], (L, F, D), F ** -0.5),
        "final_norm": gain(ks[21], (D,)),
    }

def first_block(x, c, positions, ada_w, ada_b, ffn1_norm, ffn1_w_gate, ffn1_w_up, ffn1_w_down,
              mix_norm, w_in, pool_w, pool_scale, q_a_norm, w_q_b, kv_a_norm, w_kv_b, w_out,
              ffn2_norm, ffn2_w_gate, ffn2_w_up, ffn2_w_down, final_norm):
    inv_freq = 1.0 / (ROPE_THETA ** (jnp.arange(0, QK_ROPE, 2, dtype=jnp.float32) / QK_ROPE))
    ang = positions.astype(jnp.float32)[..., None] * inv_freq
    ang = jnp.concatenate([ang, ang], axis=-1)
    cos = jnp.cos(ang).astype(x.dtype)
    sin = jnp.sin(ang).astype(x.dtype)
    c_act = jax.nn.silu(c)

    for l in range(DEPTH):
        mod = c_act @ ada_w[l] + ada_b[l]
        (sh1, sc1, g1, sh2, sc2, g2, sh3, sc3, g3) = jnp.split(mod, 3 * N_SUBLAYERS, axis=-1)

        h = modulate(rms_norm(x, ffn1_norm[l]), sh1, sc1)
        x = x + 0.5 * g1[:, None, :] * swiglu(h, ffn1_w_gate[l], ffn1_w_up[l], ffn1_w_down[l])

        h = modulate(rms_norm(x, mix_norm[l]), sh2, sc2)
        z = h @ w_in[l]
        o1 = POOL_WIDTH
        o2 = o1 + Q_LORA
        o3 = o2 + KV_LORA
        y_pool = causal_multiscale_pool(z[..., :o1], pool_w[l], pool_scale[l])
        y_mla = mla_attention(z[..., o1:o2], z[..., o2:o3], z[..., o3:], q_a_norm[l], w_q_b[l],
                              kv_a_norm[l], w_kv_b[l], cos, sin)
        y = jnp.concatenate([y_pool, y_mla], axis=-1) @ w_out[l]
        x = x + g2[:, None, :] * y

        h = modulate(rms_norm(x, ffn2_norm[l]), sh3, sc3)
        x = x + 0.5 * g3[:, None, :] * swiglu(h, ffn2_w_gate[l], ffn2_w_up[l], ffn2_w_down[l])

    return rms_norm(x, final_norm)


DEPTH_2 = 1

D_MIX = D_MODEL
D_SSM = D_MIX // 2
D_ATTN = D_MIX - D_SSM
SSM_GROUP = 16
N_SSM_GROUPS = D_SSM // SSM_GROUP
SSM_STATE = 64
DT_MIN = 1e-3
DT_MAX = 1e-1
HEAD_DIM = 64
N_HEADS_2 = D_ATTN // HEAD_DIM
MOBA_BLOCK = 256
MOBA_TOPK = 3
Q_CHUNK = 16
D_FF_2 = -(-8 * D_MODEL // (3 * 256)) * 256
RMS_EPS = 1e-6


def rmsnorm(x, g):
    xf = x.astype(jnp.float32)
    y = xf * lax.rsqrt(jnp.mean(xf * xf, axis=-1, keepdims=True) + RMS_EPS)
    return (y * g.astype(jnp.float32)).astype(x.dtype)

def _complex_affine_combine(e1, e2):
    a1r, a1i, b1r, b1i = e1
    a2r, a2i, b2r, b2i = e2
    ar = a2r * a1r - a2i * a1i
    ai = a2r * a1i + a2i * a1r
    br = a2r * b1r - a2i * b1i + b2r
    bi = a2r * b1i + a2i * b1r + b2i
    return (ar, ai, br, bi)

def s5_mixer(u, a_re, a_im, log_dt, b_re, b_im, c_re, c_im, d_skip, w_glu, b_glu):
    bsz, s, _ = u.shape
    f32 = jnp.float32
    uf = u.astype(f32).reshape(bsz, s, N_SSM_GROUPS, SSM_GROUP)
    a_re = a_re.astype(f32); a_im = a_im.astype(f32)
    dt = jnp.exp(log_dt.astype(f32))[:, None]
    mag = jnp.exp(a_re * dt)
    ang = a_im * dt
    lb_re = mag * jnp.cos(ang)
    lb_im = mag * jnp.sin(ang)
    nr = lb_re - 1.0
    den = a_re * a_re + a_im * a_im
    cr = (nr * a_re + lb_im * a_im) / den
    ci = (lb_im * a_re - nr * a_im) / den
    b_re = b_re.astype(f32); b_im = b_im.astype(f32)
    bb_re = cr[..., None] * b_re - ci[..., None] * b_im
    bb_im = cr[..., None] * b_im + ci[..., None] * b_re
    bu_re = jnp.einsum('bsgh,gph->bsgp', uf, bb_re)
    bu_im = jnp.einsum('bsgh,gph->bsgp', uf, bb_im)
    ar = jnp.broadcast_to(lb_re, (1, s) + lb_re.shape)
    ai = jnp.broadcast_to(lb_im, (1, s) + lb_im.shape)
    _, _, st_re, st_im = lax.associative_scan(
        _complex_affine_combine, (ar, ai, bu_re, bu_im), axis=1)
    y = (jnp.einsum('bsgp,ghp->bsgh', st_re, c_re.astype(f32))
         - jnp.einsum('bsgp,ghp->bsgh', st_im, c_im.astype(f32))
         + d_skip.astype(f32) * uf)
    y = jax.nn.gelu(y.reshape(bsz, s, D_SSM))
    y = y * jax.nn.sigmoid(jnp.einsum('bsc,ce->bse', y, w_glu.astype(f32)) + b_glu.astype(f32))
    return y.astype(u.dtype)

def moba_attention(q, k, v):
    bsz, s, _ = q.shape
    n_blocks = -(-s // MOBA_BLOCK)
    sp = n_blocks * MOBA_BLOCK
    k_sel = min(MOBA_TOPK, n_blocks)
    n_chunks = sp // Q_CHUNK

    def heads(t):
        t = t.astype(jnp.float32).reshape(bsz, s, N_HEADS_2, HEAD_DIM).transpose(0, 2, 1, 3)
        return jnp.pad(t, ((0, 0), (0, 0), (0, sp - s), (0, 0)))

    qh = heads(q) * (HEAD_DIM ** -0.5)
    kh = heads(k)
    vh = heads(v)
    k_blocks = kh.reshape(bsz, N_HEADS_2, n_blocks, MOBA_BLOCK, HEAD_DIM)
    v_blocks = vh.reshape(bsz, N_HEADS_2, n_blocks, MOBA_BLOCK, HEAD_DIM)
    k_mean = jnp.mean(k_blocks, axis=3)

    gate = jnp.einsum('bhsd,bhnd->bhsn', qh, k_mean)
    q_blk = jnp.arange(sp) // MOBA_BLOCK
    past = jnp.arange(n_blocks)[None, :] < q_blk[:, None]
    gate = jnp.where(past, gate, -jnp.inf)
    _, sel_idx = lax.top_k(gate, k_sel)
    sel_valid = jnp.arange(k_sel)[None, :] < q_blk[:, None]

    def to_chunks(t):
        return jnp.moveaxis(t.reshape(bsz, N_HEADS_2, n_chunks, Q_CHUNK, *t.shape[3:]), 2, 0)

    q_c = to_chunks(qh)
    idx_c = to_chunks(sel_idx)
    valid_c = sel_valid.reshape(n_chunks, Q_CHUNK, k_sel)
    gather = jax.vmap(jax.vmap(lambda blocks, ix: blocks[ix]))

    def chunk_attend(args):
        c, qc, ic, vc = args
        kg = gather(k_blocks, ic)
        vg = gather(v_blocks, ic)
        s_sel = jnp.einsum('bhqd,bhqnjd->bhqnj', qc, kg)
        s_sel = jnp.where(vc[None, None, :, :, None], s_sel, -jnp.inf)
        own = (c * Q_CHUNK) // MOBA_BLOCK
        k_own = lax.dynamic_index_in_dim(k_blocks, own, axis=2, keepdims=False)
        v_own = lax.dynamic_index_in_dim(v_blocks, own, axis=2, keepdims=False)
        s_own = jnp.einsum('bhqd,bhjd->bhqj', qc, k_own)
        q_pos = c * Q_CHUNK + jnp.arange(Q_CHUNK)
        k_pos = own * MOBA_BLOCK + jnp.arange(MOBA_BLOCK)
        s_own = jnp.where(k_pos[None, :] <= q_pos[:, None], s_own, -jnp.inf)
        scores = jnp.concatenate(
            [s_sel.reshape(bsz, N_HEADS_2, Q_CHUNK, k_sel * MOBA_BLOCK), s_own], axis=-1)
        p = jax.nn.softmax(scores, axis=-1)
        p_sel = p[..., :k_sel * MOBA_BLOCK].reshape(bsz, N_HEADS_2, Q_CHUNK, k_sel, MOBA_BLOCK)
        p_own = p[..., k_sel * MOBA_BLOCK:]
        return (jnp.einsum('bhqnj,bhqnjd->bhqd', p_sel, vg)
                + jnp.einsum('bhqj,bhjd->bhqd', p_own, v_own))

    out = lax.map(chunk_attend, (jnp.arange(n_chunks), q_c, idx_c, valid_c))
    out = out.transpose(1, 0, 3, 2, 4).reshape(bsz, sp, D_ATTN)
    return out[:, :s].astype(q.dtype)

def hybrid_layer(x, g_pre_mix, w_in, ssm_a_re, ssm_a_im, ssm_log_dt, ssm_b_re, ssm_b_im,
                 ssm_c_re, ssm_c_im, ssm_d, w_glu, b_glu, g_ssm_out, g_attn_out, w_out,
                 g_post_mix, g_pre_ffn, w_gate, w_up, w_down, g_post_ffn):
    h = rmsnorm(x, g_pre_mix)
    z = jnp.einsum('bsd,de->bse', h, w_in)
    u, q, k, v = jnp.split(z, [D_SSM, D_SSM + D_ATTN, D_SSM + 2 * D_ATTN], axis=-1)
    y_ssm = s5_mixer(u, ssm_a_re, ssm_a_im, ssm_log_dt, ssm_b_re, ssm_b_im,
                     ssm_c_re, ssm_c_im, ssm_d, w_glu, b_glu)
    y_attn = moba_attention(q, k, v)
    mix = jnp.concatenate([rmsnorm(y_ssm, g_ssm_out), rmsnorm(y_attn, g_attn_out)], axis=-1)
    x = x + rmsnorm(jnp.einsum('bse,ed->bsd', mix, w_out), g_post_mix)
    h = rmsnorm(x, g_pre_ffn)
    f = jax.nn.silu(jnp.einsum('bsd,df->bsf', h, w_gate)) * jnp.einsum('bsd,df->bsf', h, w_up)
    x = x + rmsnorm(jnp.einsum('bsf,fd->bsd', f, w_down), g_post_ffn)
    return x

def second_inputs(seed: int = 0) -> dict:
    key = jax.random.key(seed)
    ks = jax.random.split(key, 24)
    f32 = jnp.float32
    G, P, H = N_SSM_GROUPS, SSM_STATE, SSM_GROUP
    L = DEPTH_2

    def nrm(k, shape, scale):
        return jax.random.normal(k, shape, f32) * scale

    def gain(k, n):
        return 1.0 + 0.01 * jax.random.normal(k, (L, n), f32)

    n_idx = jnp.arange(P, dtype=f32)
    return dict(
        x=nrm(ks[0], (BATCH, SEQ, D_MODEL), 1.0),
        g_pre_mix=gain(ks[1], D_MODEL),
        w_in=nrm(ks[2], (L, D_MODEL, D_SSM + 3 * D_ATTN), D_MODEL ** -0.5),
        ssm_a_re=-0.5 + nrm(ks[3], (L, G, P), 0.01),
        ssm_a_im=math.pi * n_idx[None, None, :] + nrm(ks[4], (L, G, P), 0.01),
        ssm_log_dt=jax.random.uniform(ks[5], (L, G), f32, minval=math.log(DT_MIN), maxval=math.log(DT_MAX)),
        ssm_b_re=nrm(ks[6], (L, G, P, H), (2 * H) ** -0.5),
        ssm_b_im=nrm(ks[7], (L, G, P, H), (2 * H) ** -0.5),
        ssm_c_re=nrm(ks[8], (L, G, H, P), (2 * P) ** -0.5),
        ssm_c_im=nrm(ks[9], (L, G, H, P), (2 * P) ** -0.5),
        ssm_d=nrm(ks[10], (L, G, H), 1.0),
        w_glu=nrm(ks[11], (L, D_SSM, D_SSM), D_SSM ** -0.5),
        b_glu=nrm(ks[12], (L, D_SSM), 0.01),
        g_ssm_out=gain(ks[13], D_SSM),
        g_attn_out=gain(ks[14], D_ATTN),
        w_out=nrm(ks[15], (L, D_MIX, D_MODEL), D_MIX ** -0.5),
        g_post_mix=gain(ks[16], D_MODEL),
        g_pre_ffn=gain(ks[17], D_MODEL),
        w_gate=nrm(ks[18], (L, D_MODEL, D_FF_2), D_MODEL ** -0.5),
        w_up=nrm(ks[19], (L, D_MODEL, D_FF_2), D_MODEL ** -0.5),
        w_down=nrm(ks[20], (L, D_FF_2, D_MODEL), D_FF_2 ** -0.5),
        g_post_ffn=gain(ks[21], D_MODEL),
    )

def second_block(x, g_pre_mix, w_in, ssm_a_re, ssm_a_im, ssm_log_dt, ssm_b_re, ssm_b_im,
              ssm_c_re, ssm_c_im, ssm_d, w_glu, b_glu, g_ssm_out, g_attn_out, w_out,
              g_post_mix, g_pre_ffn, w_gate, w_up, w_down, g_post_ffn):
    for l in range(DEPTH_2):
        x = hybrid_layer(x, g_pre_mix[l], w_in[l], ssm_a_re[l], ssm_a_im[l], ssm_log_dt[l],
                         ssm_b_re[l], ssm_b_im[l], ssm_c_re[l], ssm_c_im[l], ssm_d[l],
                         w_glu[l], b_glu[l], g_ssm_out[l], g_attn_out[l], w_out[l],
                         g_post_mix[l], g_pre_ffn[l], w_gate[l], w_up[l], w_down[l], g_post_ffn[l])
    return x


_first_inputs = second_inputs


def second_inputs(seed=0):
    import zlib

    import numpy as np

    out = dict(_first_inputs(seed))
    spreads = {}
    factors = {'g_pre_mix': 4.4,
     'ssm_a_re': 64.0,
     'b_glu': 27.917,
     'g_ssm_out': 54.538,
     'g_attn_out': 54.665,
     'g_post_mix': 32.269,
     'g_pre_ffn': 37.171,
     'g_post_ffn': 58.642,
     'ssm_b_re': 3.03,
     'ssm_b_im': 3.014,
     'ssm_c_re': 3.039,
     'ssm_c_im': 3.015}
    for name, (base, spread) in spreads.items():
        noise = np.random.default_rng([zlib.crc32(name.encode()), seed]).standard_normal(out[name].shape)
        drawn = base * np.exp(spread * noise) if base else spread * noise
        out[name] = __import__('jax').numpy.asarray(drawn.astype(out[name].dtype))
    for name, factor in factors.items():
        out[name] = (out[name] * factor).astype(out[name].dtype)
    return out


_narrow_inputs = second_inputs


def second_inputs(seed=0):

    out = dict(_narrow_inputs(seed))
    wider = {'ssm_a_re': 12.0,
     'g_ssm_out': 7.17,
     'g_attn_out': 7.18,
     'g_post_mix': 4.86,
     'g_pre_ffn': 5.24,
     'g_post_ffn': 7.06}
    for name, times in wider.items():
        mean = out[name].mean()
        out[name] = (mean + times * (out[name] - mean)).astype(out[name].dtype)
    return out


def setup_inputs(seed=0):
    out = dict(first_inputs(seed))
    for name, value in second_inputs(seed + 1).items():
        if name != "x":
            out[name + "_2"] = value
    return out


def reference(
    x, c, positions, ada_w, ada_b, ffn1_norm, ffn1_w_gate, ffn1_w_up, ffn1_w_down, mix_norm,
    w_in, pool_w, pool_scale, q_a_norm, w_q_b, kv_a_norm, w_kv_b, w_out, ffn2_norm, ffn2_w_gate,
    ffn2_w_up, ffn2_w_down, final_norm, g_pre_mix_2, w_in_2, ssm_a_re_2, ssm_a_im_2,
    ssm_log_dt_2, ssm_b_re_2, ssm_b_im_2, ssm_c_re_2, ssm_c_im_2, ssm_d_2, w_glu_2, b_glu_2,
    g_ssm_out_2, g_attn_out_2, w_out_2, g_post_mix_2, g_pre_ffn_2, w_gate_2, w_up_2, w_down_2,
    g_post_ffn_2,
):
    x = first_block(
        x, c, positions, ada_w, ada_b, ffn1_norm, ffn1_w_gate, ffn1_w_up, ffn1_w_down, mix_norm,
        w_in, pool_w, pool_scale, q_a_norm, w_q_b, kv_a_norm, w_kv_b, w_out, ffn2_norm,
        ffn2_w_gate, ffn2_w_up, ffn2_w_down, final_norm,
    )
    return second_block(
        x, g_pre_mix_2, w_in_2, ssm_a_re_2, ssm_a_im_2, ssm_log_dt_2, ssm_b_re_2, ssm_b_im_2,
        ssm_c_re_2, ssm_c_im_2, ssm_d_2, w_glu_2, b_glu_2, g_ssm_out_2, g_attn_out_2, w_out_2,
        g_post_mix_2, g_pre_ffn_2, w_gate_2, w_up_2, w_down_2, g_post_ffn_2,
    )


_drawn_inputs = setup_inputs


def setup_inputs(seed=0):
    import zlib

    import numpy as np

    out = dict(_drawn_inputs(seed))
    spreads = {}
    factors = {'q_a_norm': 3.371, 'ssm_a_re_2': 2.887}
    for name, (base, spread) in spreads.items():
        noise = np.random.default_rng([zlib.crc32(name.encode()), seed]).standard_normal(out[name].shape)
        drawn = base * np.exp(spread * noise) if base else spread * noise
        out[name] = __import__('jax').numpy.asarray(drawn.astype(out[name].dtype))
    for name, factor in factors.items():
        out[name] = (out[name] * factor).astype(out[name].dtype)
    return out
```

```python
import math
from contextlib import ExitStack

import numpy as np

import concourse.bass as bass
from concourse import mybir

F32 = mybir.dt.float32
F32R = mybir.dt.float32r
I32 = mybir.dt.int32
ALU = mybir.AluOpType
ACT = mybir.ActivationFunctionType
AX = mybir.AxisListType

P = 128
D = 1024
S = 256
TT = S // P
KC = D // P
FF = 2816
FB = FF // P
DEPTH = 2
NFFN = 2 * DEPTH + 1
EPS = 1e-6

HEADS = 4
POOLG = 4
QCH, KVCH = 3, 2
MLA_SCALE = 1.0 / math.sqrt(192)
ZT = 11
TILES = 37
UNITS = 25
PADT = 16

HEADS2, HD2 = 8, 64
ST = 16
UT = 4
UNITS2 = 26

RING = 4
MASKED = -1e30
TWO_PI = 2 * math.pi
ROUND = 12582912.0

C_C, C_FREQ, C_SIGN, C_ARE, C_AIM, C_DT, C_RATIO = 0, 8, 9, 10, 26, 42, 58
C_MASK = C_RATIO + 4 * PADT
C_ID = C_MASK + 384
C_BRE = C_ID + P
C_BIM, C_CRE, C_CIM = C_BRE + 256, C_BRE + 512, C_BRE + 768
C_N = C_BRE + 1024
L_ADA, L_NORM, L_PSC, L_QN, L_KVN, L_N = 0, 48, 72, 76, 79, 81
B_MIX, B_FFN, B_SSM, B_ATT, B_GLU, B_SKIP = 0, 8, 16, 20, 24, 28


def split_two_pi(parts, bits):
    rest, out = TWO_PI, []
    for n in range(parts):
        if n == parts - 1:
            out.append(float(np.float32(rest)))
        else:
            scale = 2.0 ** (bits - 1 - math.floor(math.log2(rest)))
            out.append(math.floor(rest * scale) / scale)
        rest -= out[-1]
    return out


class Steps:

    def __init__(self, engine, sem):
        self.engine, self.sem, self.base, self.n = engine, sem, 0, 0

    def did(self, instruction):
        instruction.then_inc(self.sem, 1)
        self.n += 1

    def settle(self):
        self.engine.wait_ge(self.sem, self.base + self.n)

    def then(self, instruction):
        self.did(instruction)
        self.settle()

    def enter_layers(self, layer, per_layer):
        self.before = self.base + self.n
        self.base, self.n, self.per_layer = self.before + layer * per_layer, 0, per_layer

    def leave_layers(self):
        assert self.n == self.per_layer, (self.n, self.per_layer)
        self.base, self.n = self.before + DEPTH * self.per_layer, 0


DVE_LAYER = 54
ACT_LAYER = 6


def program(nc, x_in, positions, consts, cols, gate_rows, rows, ada, ffn_gu, ffn_dn, mix_w, mix2_w, out):
    ctx = ExitStack()
    with ctx:
        def sem(name):
            return ctx.enter_context(nc.semaphore(name))

        def bank(name):
            return ctx.enter_context(nc.psum_tensor(name, [P, 512], F32))

        def sb(stack, name, shape, dt=F32):
            return stack.enter_context(nc.sbuf_tensor(name, shape, dt))

        x = sb(ctx, "x", [P, TT, D])
        xn = sb(ctx, "xn", [P, TT, D])
        hT = sb(ctx, "hT", [P, KC, S])
        raw_gu = sb(ctx, "raw_gu", [P, 2, 2 * KC * P])
        raw_dn = sb(ctx, "raw_dn", [P, 2, D])
        ring = sb(ctx, "ring", [P, RING, D])
        gate_b = sb(ctx, "gate_b", [P, D])
        cst = sb(ctx, "cst", [P, C_N])
        lc = sb(ctx, "lc", [P, L_N])
        cosT = sb(ctx, "cosT", [P, S])
        sinT = sb(ctx, "sinT", [P, S])
        ones = sb(ctx, "ones", [P, P])
        tiny = sb(ctx, "tiny", [P, 2])
        c_act = sb(ctx, "c_act", [P, KC])
        mods = sb(ctx, "mods", [P, 16])
        gs = sb(ctx, "gs", [P, KC])
        ss = sb(ctx, "ss", [P, 4])
        rms = sb(ctx, "rms", [P, 2])
        rstd = sb(ctx, "rstd", [P, 2])
        mag = sb(ctx, "mag", [P, ST])
        cos1 = sb(ctx, "cos1", [P, ST])
        sin1 = sb(ctx, "sin1", [P, ST])
        cre = sb(ctx, "cre", [P, ST])
        cim = sb(ctx, "cim", [P, ST])
        cz = sb(ctx, "cz", [P, 3, ST, 2, 16])
        sp = sb(ctx, "sp", [P, 8, ST])
        ident = cst[:, C_ID:C_ID + P]
        mask = cst[:, C_MASK:C_MASK + 384]

        area = ExitStack()
        ada_in = sb(area, "ada_in", [P, 2, KC, S])
        part = sb(area, "part", [P, 7, D])
        area.close()
        ecos = sb(ctx, "ecos", [P, ST, S])
        esin = sb(ctx, "esin", [P, ST, S])
        bbd = sb(ctx, "bbd", [P, 2, UT, 4, 2, 16])
        mixT2 = sb(ctx, "mixT2", [P, KC, S])
        work = ExitStack()
        pro = sb(work, "pro", [P, 8, KC, S])
        work.close()
        work = ExitStack()
        gu_hi = sb(work, "gu_hi", [P, 2, 2, KC, P], F32R)
        gu_lo = sb(work, "gu_lo", [P, 2, 2, KC, P], F32R)
        dn_hi = sb(work, "dn_hi", [P, 2, D], F32R)
        dn_lo = sb(work, "dn_lo", [P, 2, D], F32R)
        hT_hi = sb(work, "hT_hi", [P, KC, S], F32R)
        hT_lo = sb(work, "hT_lo", [P, KC, S], F32R)
        sg = sb(work, "sg", [P, 2, S])
        prod = sb(work, "prod", [P, 2, S])
        act_hi = sb(work, "act_hi", [P, 2, S], F32R)
        act_lo = sb(work, "act_lo", [P, 2, S], F32R)
        work.close()
        work = ExitStack()
        z = sb(work, "z", [P, 7, S])
        sq = sb(work, "sq", [P, QCH + KVCH, S])
        lat_rms = sb(work, "lat_rms", [P, 2, S])
        latn = sb(work, "latn", [P, QCH + KVCH, S])
        qn = sb(work, "qn", [P, HEADS, S])
        qrs = sb(work, "qrs", [P, 4, S])
        qr = sb(work, "qr", [P, 2, S])
        krz = sb(work, "krz", [P, 2, S])
        kn = sb(work, "kn", [P, HEADS, S])
        v = sb(work, "v", [P, TT, HEADS * P])
        pm = sb(work, "pm", [P, HEADS, 384])
        pT = sb(work, "pT", [P, HEADS, 384])
        mixT = sb(work, "mixT", [P, KC, S])
        upad = sb(work, "upad", [P, POOLG, PADT + S])
        sumA = sb(work, "sumA", [P, POOLG, PADT + S])
        sumB = sb(work, "sumB", [P, POOLG - 1, PADT + S])
        rot = sb(work, "rot", [P, 2, 2, S])
        rmax = sb(work, "rmax", [P, HEADS, 2])
        negm = sb(work, "negm", [P, HEADS, 2])
        psum_ = sb(work, "psums", [P, HEADS, 2])
        prec = sb(work, "prec", [P, HEADS, 2])
        work.close()
        work = ExitStack()
        u2 = sb(work, "u2", [P, UT, S])
        q2 = sb(work, "q2", [P, UT, S])
        kz = sb(work, "kz", [P, HEADS2, S])
        v2 = sb(work, "v2", [P, TT, 512])
        pm2 = sb(work, "pm2", [P, HEADS2, 384])
        pT2 = sb(work, "pT2", [P, 4, 384])
        bbT = sb(work, "bbT", [P, 2, UT, P])
        ma = sb(work, "ma", [P, 2, S])
        mb = sb(work, "mb", [P, 2, S])
        vin = sb(work, "vin", [P, 2, S])
        ysc = sb(work, "ysc", [P, 3, 2, S])
        mc = sb(work, "mc", [P, 2, 2, S])
        ms = sb(work, "ms", [P, 2, 2, S])
        y2 = sb(work, "y2", [P, UT, S])
        sig = sb(work, "sig", [P, UT, S])
        sq2 = q2
        rmax2 = sb(work, "rmax2", [P, HEADS2, 2])
        negm2 = sb(work, "negm2", [P, HEADS2, 2])
        psum2 = sb(work, "psums2", [P, 2, HEADS2])
        prec2 = sb(work, "prec2", [P, 2, HEADS2])
        rmsT = sb(work, "rmsT", [P, S])
        rstdT = sb(work, "rstdT", [P, S])
        row_b = sb(work, "row_b", [P, D])
        work.close()
        pos_i = xn[:, 1, 0:S].bitcast(I32)
        work = ExitStack()
        sb(work, "behind", [P, 18 * 1024])
        rot4 = sb(work, "rot4", [P, 2, 2, P])
        wpow = sb(work, "wpow", [P, 6, ST])
        final_b = sb(work, "final_b", [P, D])
        work.close()

        gu_bank = [bank("gu_bank0"), bank("gu_bank1")]
        yb = [bank(f"y_bank{n}") for n in range(4)]
        tb = [bank("t_bank0"), bank("t_bank1")]
        zb = [*gu_bank, *tb]

        x_loaded, cst_loaded, pos_loaded, lc_loaded = sem("x_loaded"), sem("cst_loaded"), sem("pos_loaded"), sem("lc_loaded")
        pro_loaded = [sem(f"pro_loaded{n}") for n in range(8)]
        ada_loaded = [sem("ada_loaded0"), sem("ada_loaded1")]
        gu_loaded = [sem("gu_loaded0"), sem("gu_loaded1")]
        dn_loaded = [sem("dn_loaded0"), sem("dn_loaded1")]
        unit_loaded = [sem(f"unit_loaded{n}") for n in range(RING)]
        gbias_loaded, row_loaded, final_loaded, stored = sem("gbias_loaded"), sem("row_loaded"), sem("final_loaded"), sem("stored")
        dve_step, act_step, pool_step = sem("dve_step"), sem("act_step"), sem("pool_step")
        ones_set, c_ready, pro_done, pro_pool = sem("ones_set"), sem("c_ready"), sem("pro_done"), sem("pro_pool")
        prep_act, prep_args, prep_dve = sem("prep_act"), sem("prep_args"), sem("prep_dve")
        ada_step, piece_done = sem("ada_step"), sem("piece_done")
        mod_ps, mod_done, gate_ps, gate_done = sem("mod_ps"), sem("mod_done"), sem("gate_ps"), sem("gate_done")
        x_ready, rms_ready, xn_ready, tr_ready, hT_ready = sem("x_ready"), sem("rms_ready"), sem("xn_ready"), sem("tr_ready"), sem("hT_ready")
        hT_hi_done, hT_lo_done = sem("hT_hi_done"), sem("hT_lo_done")
        gu_hi_done, gu_lo_done, dn_hi_done, dn_lo_done = sem("gu_hi_done"), sem("gu_lo_done"), sem("dn_hi_done"), sem("dn_lo_done")
        gu_ps, silu_done, prod_done, act_hi_done, act_done, dn_used, y_ps = (
            sem("gu_ps"), sem("silu_done"), sem("prod_done"), sem("act_hi_done"), sem("act_done"), sem("dn_used"), sem("y_ps"))
        tile_ps, tile_out, wout_done = sem("tile_ps"), sem("tile_out"), sem("wout_done")
        sq_ready, lat_ss, lat_rooted, lat_done = sem("sq_ready"), sem("lat_ss"), sem("lat_rooted"), sem("lat_done")
        kr_ready, qr_ready, diff_ready = sem("kr_ready"), sem("qr_ready"), sem("diff_ready")
        sc_ps, negm_ready, p_ready, pn_ready = sem("sc_ps"), sem("negm_ready"), sem("p_ready"), sem("pn_ready")
        tables_done, bb_ps, bb_done, bu_ps, bu_used, scanned, turned, c_ps, skip_done = (
            sem("tables_done"), sem("bb_ps"), sem("bb_done"), sem("bu_ps"), sem("bu_used"), sem("scanned"), sem("turned"), sem("c_ps"), sem("skip_done"))
        gelu_done, glu_ps, sig_done, glu_done, sq2_done, ssm_ss, ssm_rooted, ssm_done = (
            sem("gelu_done"), sem("glu_ps"), sem("sig_done"), sem("glu_done"), sem("sq2_done"), sem("ssm_ss"), sem("ssm_rooted"), sem("ssm_done"))
        sc2_ps, sm2_done, negm2_done, p2_done, pt_ps, pt_out, o_ps, o_done, o_rooted, on_done, ot_ps, att_done, kz_zero = (
            sem("sc2_ps"), sem("sm2_done"), sem("negm2_done"), sem("p2_done"), sem("pt_ps"), sem("pt_out"), sem("o_ps"), sem("o_done"),
            sem("o_rooted"), sem("on_done"), sem("ot_ps"), sem("att_done"), sem("kz_zero"))
        post_ss, post_rooted = sem("post_ss"), sem("post_rooted")

        block = ctx.enter_context(nc.Block())

        def half(b):
            return slice(512 * b, 512 * (b + 1))

        def tok(t):
            return slice(P * t, P * (t + 1))

        NORMS = 3 * DEPTH

        @block.sync
        def _(sp_):
            def load_gu(g, b):
                sp_.dma_start(raw_gu[:, b, :], ffn_gu[bass.ds(g, 1)].rearrange("a p n -> p (a n)")).then_inc(gu_loaded[b], 16)

            def load_dn(g, b):
                sp_.dma_start(raw_dn[:, b, :], ffn_dn[bass.ds(g, 1)].rearrange("a p n -> p (a n)")).then_inc(dn_loaded[b], 16)

            def gate_bias(k, row):
                sp_.wait_ge(x_ready, 4 * k + 4)
                sp_.dma_start(gate_b[:, :], gate_rows[bass.ds(row, 1)].to_broadcast([P, D])).then_inc(gbias_loaded, 16)

            def ffn_loads(base, blocks):
                with sp_.Fori(0, blocks // 2) as i:
                    for b in range(2):
                        sp_.wait_ge(gu_lo_done, base + 2 * i + b + 1)
                        load_gu(base + 2 * i + b + 2, b)
                        sp_.wait_ge(dn_lo_done, base + 2 * i + b + 1)
                        load_dn(base + 2 * i + b + 2, b)

            def units(src, at, count, used):
                for n in range(count):
                    if n >= RING:
                        sp_.wait_ge(*used(n - RING))
                    sp_.dma_start(ring[:, n % RING, :], src[bass.ds(at + n, 1)].rearrange("a p n -> p (a n)"))\
                       .then_inc(unit_loaded[n % RING], 16)

            def mixer_used(l):
                tiles = [*range(1, ZT + 1), *[ZT + 8] * QCH, *[ZT + 8 + HEADS + TT] * KVCH, ZT + 8 + HEADS + TT + POOLG]

                def used(n):
                    if n < len(tiles):
                        return tile_ps, TILES * l + tiles[n]
                    return wout_done, (KC - 1) * l + n - len(tiles) + 1
                return used

            def mixer2_used(n):
                if n < 16:
                    return tile_ps, TILES * DEPTH + min(n + 1, 12) + TT * (n >= 12)
                if n < 18:
                    return glu_ps, UT
                return wout_done, (KC - 1) * DEPTH + n - 17

            sp_.dma_start(cst[:, :], consts).then_inc(cst_loaded, 16)
            sp_.dma_start(pos_i, positions.to_broadcast([P, S])).then_inc(pos_loaded, 16)
            sp_.dma_start(lc[:, :], cols[0]).then_inc(lc_loaded, 16)
            for n in range(8):
                sp_.dma_start(pro[:, n, :, :], ada[n].rearrange("p (c n) -> p c n", c=KC)).then_inc(pro_loaded[n], 16)
                if n == 3:
                    sp_.dma_start(x[:, :, :], x_in.rearrange("(t p) d -> p t d", p=P)).then_inc(x_loaded, 16)
            for g in range(2):
                load_gu(g, g)
                load_dn(g, g)
            with sp_.Fori(0, DEPTH) as l:
                gate_bias(3 * l, 3 * l)
                ffn_loads(2 * FB * l, FB)
                gate_bias(3 * l + 1, 3 * l + 1)
                units(mix_w, UNITS * l, UNITS, mixer_used(l))
                gate_bias(3 * l + 2, 3 * l + 2)
                sp_.wait_ge(mod_done, 3 * l + 3)
                sp_.dma_start(lc[:, :], cols[bass.ds(l + 1, 1)].rearrange("a p n -> p (a n)")).then_inc(lc_loaded, 16)
                ffn_loads(2 * FB * l + FB, FB)
            sp_.dma_start(final_b[:, :], rows[0:1].to_broadcast([P, D])).then_inc(final_loaded, 16)
            units(mix2_w, 0, UNITS2, mixer2_used)
            sp_.wait_ge(x_ready, 4 * NORMS + 4)
            sp_.dma_start(row_b[:, :], rows[1:2].to_broadcast([P, D])).then_inc(row_loaded, 16)
            sp_.dma_start(gate_b[:, :], rows[2:3].to_broadcast([P, D])).then_inc(gbias_loaded, 16)
            ffn_loads(4 * FB, FB - 2)
            for t in range(TT):
                sp_.wait_ge(x_ready, 4 * NORMS + 14 + 2 * t)
                sp_.dma_start(out.rearrange("(t p) d -> p t d", p=P)[:, t, :], x[:, t, :]).then_inc(stored, 16)
            sp_.wait_ge(stored, 32)

        @block.gpsimd
        def _(pool):
            step = Steps(pool, pool_step)
            pool.memset(ones[:, :], 1.0).then_inc(ones_set, 1)
            pool.memset(tiny[:, 0:1], EPS).then_inc(ones_set, 1)
            pool.memset(tiny[:, 1:2], math.pi / 2).then_inc(ones_set, 1)

            def fetch(q, b):
                pool.dma_start(ada_in[:, b, :, :], ada[bass.ds(q + 8, 1)].rearrange("a p (c n) -> p (a c) n", c=KC))\
                    .then_inc(ada_loaded[b], 16)

            def weigh(chunk, add_up, into):
                add_up(pool.tensor_tensor(chunk, chunk, c_act[:, :].unsqueeze(2).to_broadcast([P, KC, S]), ALU.mult))
                add_up(pool.tensor_tensor(chunk[:, 0:4, :], chunk[:, 0:4, :], chunk[:, 4:8, :], ALU.add))
                add_up(pool.tensor_tensor(chunk[:, 0:2, :], chunk[:, 0:2, :], chunk[:, 2:4, :], ALU.add))
                return pool.tensor_tensor(into, chunk[:, 0, :], chunk[:, 1, :], ALU.add)

            pool.wait_ge(c_ready, 1)
            for n in (6, 7):
                pool.wait_ge(pro_loaded[n], 16)
                weigh(pro[:, n, :, :], step.then, part[:, 1, S * (n - 4):S * (n - 3)]).then_inc(pro_pool, 1)
            pool.sem_inc(piece_done, 1)
            for b in range(2):
                fetch(b, b)

            order = []
            for l in range(DEPTH):
                order += [(4, gate_ps, 6 * l - 4), (2, mod_ps, 3 * l - 1), (3, mod_ps, 3 * l - 1), (5, gate_ps, 6 * l - 2),
                          (0, mod_ps, 3 * l + 1), (1, mod_ps, 3 * l + 1), (6, gate_ps, 6 * l)]
                if l < DEPTH - 1:
                    order += [(0, mod_ps, 3 * l + 3), (1, mod_ps, 3 * l + 3)]
            for n, (slot, used, count) in enumerate(order):
                if count > 0:
                    pool.wait_ge(used, count)

                def chunk(i, b, more):
                    q = 4 * n + 2 * i + b
                    done = [0]

                    def own(instruction):
                        instruction.then_inc(ada_step, 1)
                        done[0] += 1
                        pool.wait_ge(ada_step, 4 * q + done[0])

                    pool.wait_ge(ada_loaded[b], 32 * n + 16 * i + 16)
                    own(weigh(ada_in[:, b, :, :], own, part[:, slot, bass.ds(2 * S * i + S * b, S)]))
                    if more:
                        fetch(q + 2, b)

                if n < len(order) - 1:
                    with pool.Fori(0, 2) as i:
                        for b in range(2):
                            chunk(i, b, True)
                else:
                    for i in range(2):
                        for b in range(2):
                            chunk(i, b, i == 0)
                pool.sem_inc(piece_done, 1)

            pool.wait_ge(mod_ps, 3 * DEPTH)
            pool.wait_ge(gate_ps, 6 * DEPTH - 2)
            pool.wait_ge(prep_dve, 1)
            step.did(pool.memset(bbd[:, :, :, :, :, :], 0.0))
            step.then(pool.memset(cz[:, :, :, :, :], 0.0))
            bre, bim = (cst[:, c:c + 256].rearrange("p (s h) -> p s h", h=16) for c in (C_BRE, C_BIM))
            c_re, c_im = (cst[:, c:c + 256].rearrange("p (s h) -> p s h", h=16) for c in (C_CRE, C_CIM))
            t1 = ecos[:, 0, :].rearrange("p (s h) -> p s h", h=16)
            t2 = ecos[:, 1, :].rearrange("p (s h) -> p s h", h=16)
            wide = [P, ST, 16]
            for r, (fr, fi, op) in enumerate(((bre, bim, ALU.subtract), (bim, bre, ALU.add))):
                step.did(pool.tensor_tensor(t1, fr, cre[:, :].unsqueeze(2).to_broadcast(wide), ALU.mult))
                step.then(pool.tensor_tensor(t2, fi, cim[:, :].unsqueeze(2).to_broadcast(wide), ALU.mult))
                for g in range(2):
                    rows_ = slice(64 * g, 64 * g + 64)
                    to = bbd[rows_, r, :, :, g, :].rearrange("p u j h -> p (u j) h")
                    step.then(pool.tensor_tensor(to, t1[rows_], t2[rows_], op))
            for n, (src, sign) in enumerate(((c_re, 1.0), (c_re, -1.0), (c_im, -1.0))):
                for g in range(2):
                    rows_ = slice(64 * g, 64 * g + 64)
                    step.then(pool.tensor_scalar(cz[rows_, n, :, g, :], src[rows_], sign, None, ALU.mult))
            step.did(pool.memset(ecos[:, :, 0:1], 1.0))
            step.did(pool.memset(esin[:, :, 0:1], 0.0))
            step.did(pool.tensor_copy(wpow[:, 0, :], cos1[:, :]))
            step.then(pool.tensor_copy(wpow[:, 1, :], sin1[:, :]))
            n = 1
            while n < S:
                for s in range(0, ST, 2):
                    e_c, e_s = ecos[:, s:s + 2, 0:n], esin[:, s:s + 2, 0:n]
                    w_c, w_s = (wpow[:, a, s:s + 2].unsqueeze(2).to_broadcast([P, 2, n]) for a in (0, 1))
                    o1, o2 = rot4[:, 0, :, 0:n], rot4[:, 1, :, 0:n]
                    step.did(pool.tensor_tensor(o1, e_c, w_c, ALU.mult))
                    step.then(pool.tensor_tensor(o2, e_s, w_s, ALU.mult))
                    step.then(pool.tensor_tensor(ecos[:, s:s + 2, n:2 * n], o1, o2, ALU.subtract))
                    step.did(pool.tensor_tensor(o1, e_c, w_s, ALU.mult))
                    step.then(pool.tensor_tensor(o2, e_s, w_c, ALU.mult))
                    step.then(pool.tensor_tensor(esin[:, s:s + 2, n:2 * n], o1, o2, ALU.add))
                step.did(pool.tensor_tensor(wpow[:, 2, :], wpow[:, 0, :], wpow[:, 0, :], ALU.mult))
                step.did(pool.tensor_tensor(wpow[:, 3, :], wpow[:, 1, :], wpow[:, 1, :], ALU.mult))
                step.then(pool.tensor_tensor(wpow[:, 4, :], wpow[:, 0, :], wpow[:, 1, :], ALU.mult))
                step.did(pool.tensor_tensor(wpow[:, 0, :], wpow[:, 2, :], wpow[:, 3, :], ALU.subtract))
                step.then(pool.tensor_tensor(wpow[:, 1, :], wpow[:, 4, :], wpow[:, 4, :], ALU.add))
                n *= 2
            pool.sem_inc(tables_done, 1)

            pool.wait_ge(x_ready, 4 * NORMS + 4)
            for h in range(HEADS2):
                pool.memset(kz[64 * (1 - h % 2):64 * (2 - h % 2), h, :], 0.0).then_inc(kz_zero, 1)
                pool.wait_ge(kz_zero, h + 1)
            for s in range(ST):
                pool.wait_ge(scanned, s + 1)
                if s >= 2:
                    pool.wait_ge(c_ps, s - 1)
                for to, table in ((mc, ecos), (ms, esin)):
                    pool.tensor_tensor(to[:, s % 2, :, :], ysc[:, s % 3, :, :],
                                       table[:, s, :].unsqueeze(1).to_broadcast([P, 2, S]), ALU.mult).then_inc(turned, 1)

        @block.tensor
        def _(pe):
            def modulation(k, l, m):
                if m == 0:
                    pe.wait_ge(pro_done, 6)
                    pe.wait_ge(pro_pool, 2)
                pe.wait_ge(piece_done, 9 * l + 3 * m + 1)
                pe.wait_ge(gate_done, 2 * k + 2)
                for j in range(16):
                    last = pe.matmul(tb[0][:, j:j + 1], part[:, 2 * (m == 1) + j // KC, tok(j % KC)], ones[:, 0:1], start=True, stop=True)
                last.then_inc(mod_ps, 1)

            def transposes(k):
                for t in range(TT):
                    pe.wait_ge(xn_ready, 2 * k + t + 1)
                    for c in range(KC):
                        last = pe.transpose(yb[c // 2][:, S * (c % 2) + P * t:S * (c % 2) + P * (t + 1)], xn[:, t, tok(c)], ident)
                        if t == TT - 1 and c % 2:
                            last.then_inc(tr_ready, 1)

            def gate(l, m):
                pe.wait_ge(piece_done, 9 * l + 3 * m + 2)
                for b in range(2):
                    pe.matmul(tb[b][:, :], ones[:, :], part[:, 4 + m, half(b)], start=True, stop=True).then_inc(gate_ps, 1)

            def ffn(f, before_last):
                base = FB * f

                def gate_up(n, b, n_first=None):
                    pe.wait_ge(gu_lo_done, base + n + 1)
                    if n_first is None:
                        pe.wait_ge(prod_done, base + n - 1)
                    for h in range(2):
                        for c in range(KC):
                            if n_first == 0 and h == 0 and c % 2 == 0:
                                pe.wait_ge(hT_lo_done, 4 * f + c // 2 + 1)
                            to = gu_bank[b][:, S * h:S * (h + 1)]
                            pe.matmul(to, gu_hi[:, b, h, c, :], hT_hi[:, c, :], start=c == 0, stop=False)
                            pe.matmul(to, gu_hi[:, b, h, c, :], hT_lo[:, c, :], start=False, stop=False)
                            last = pe.matmul(to, gu_lo[:, b, h, c, :], hT_hi[:, c, :], start=False, stop=c == KC - 1)
                    last.then_inc(gu_ps, 1)

                def down(n, b, first=False, final=False):
                    pe.wait_ge(dn_lo_done, base + n + 1)
                    pe.wait_ge(act_done, base + n + 1)
                    for t in range(TT):
                        for h in range(2):
                            to = yb[2 * t + h][:, :]
                            pe.matmul(to, act_hi[:, b, tok(t)], dn_hi[:, b, half(h)], start=first, stop=False)
                            pe.matmul(to, act_hi[:, b, tok(t)], dn_lo[:, b, half(h)], start=False, stop=False)
                            last = pe.matmul(to, act_lo[:, b, tok(t)], dn_hi[:, b, half(h)], start=False, stop=final)
                            if final:
                                last.then_inc(y_ps, 1)
                    if not final:
                        last.then_inc(dn_used, 1)

                gate_up(0, 0, 0)
                gate_up(1, 1, 1)
                down(0, 0, first=True)
                with pe.Fori(0, FB // 2 - 1) as i:
                    for b in range(2):
                        gate_up(2 * i + b + 2, b)
                        down(2 * i + b + 1, 1 - b)
                before_last()
                down(FB - 1, 1, final=True)

            def mixer(l):
                base = TILES * l
                seen = [0]

                def unit(n):
                    pe.wait_ge(unit_loaded[n % RING], 16 * (-(-(UNITS - n % RING) // RING) * l + n // RING + 1))
                    return ring[:, n % RING, :]

                def tile_bank():
                    n = seen[0]
                    seen[0] += 1
                    if n >= 4:
                        pe.wait_ge(tile_out, base + n - 3)
                    return zb[n % 4]

                def z_tile(n):
                    w, to = unit(n).rearrange("p (c n) -> p c n", c=KC), tile_bank()
                    for c in range(KC):
                        last = pe.matmul(to[:, 0:S], w[:, c, :], hT[:, c, :], start=c == 0, stop=c == KC - 1)
                    last.then_inc(tile_ps, 1)

                pe.wait_ge(hT_ready, 8 * (3 * l + 1) + 8)
                for n in range(7):
                    z_tile(n)
                for a, (first, count) in enumerate(((0, QCH), (QCH, KVCH))):
                    pe.wait_ge(sq_ready, (QCH + KVCH) * l + first + count)
                    for c in range(first, first + count):
                        last = pe.matmul(yb[a][:, 0:S], ones[:, :], sq[:, c, :], start=c == first, stop=c == first + count - 1)
                    last.then_inc(lat_ss, 1)
                for n in range(7, ZT):
                    z_tile(n)

                wq = [unit(ZT + c) for c in range(QCH)]
                pe.wait_ge(lat_done, (QCH + KVCH) * l + QCH)
                for n in range(8):
                    to = tile_bank()
                    for c in range(QCH):
                        last = pe.matmul(to[:, 0:S], wq[c][:, tok(n)], latn[:, c, :], start=c == 0, stop=c == QCH - 1)
                    last.then_inc(tile_ps, 1)
                wkv = [unit(ZT + QCH + c) for c in range(KVCH)]
                pe.wait_ge(lat_done, (QCH + KVCH) * (l + 1))
                for n in range(HEADS):
                    to = tile_bank()
                    for c in range(KVCH):
                        last = pe.matmul(to[:, 0:S], wkv[c][:, tok(n)], latn[:, QCH + c, :], start=c == 0, stop=c == KVCH - 1)
                    last.then_inc(tile_ps, 1)
                for t in range(TT):
                    to = tile_bank()
                    for c in range(KVCH):
                        last = pe.matmul(to[:, :], latn[:, QCH + c, tok(t)], wkv[c][:, half(1)], start=c == 0, stop=c == KVCH - 1)
                    last.then_inc(tile_ps, 1)

                pe.wait_ge(tile_out, base + ZT + 8 + HEADS)
                pe.wait_ge(kr_ready, 2 * l + 2)
                pe.wait_ge(qr_ready, l + 1)
                pe.wait_ge(lat_rooted, 2 * l + 2)
                for h in range(HEADS):
                    for t in range(TT):
                        to = yb[h][:, 0:P] if t == 0 else yb[h][:, P:P + S]
                        keys = slice(0, P * (t + 1))
                        pe.matmul(to, qn[:, h, tok(t)], kn[:, h, keys], start=True, stop=False)
                        last = pe.matmul(to, qr[:, h // 2, tok(t)], krz[:, h % 2, keys], start=False, stop=True)
                    last.then_inc(sc_ps, 1)
                pw = unit(ZT + QCH + KVCH)
                pe.wait_ge(diff_ready, POOLG * l + POOLG)
                for g, sums in enumerate((sumA[:, 0], sumB[:, 0], sumA[:, 2], sumB[:, 2])):
                    to = tile_bank()
                    pe.matmul(to[:, 0:S], pw[:, tok(g)], sums[:, PADT:PADT + S], start=True, stop=True).then_inc(tile_ps, 1)

                def turn(h):
                    to = tile_bank()
                    pe.wait_ge(pn_ready, 2 * HEADS * l + 2 * h + 2)
                    for c in range(3):
                        last = pe.transpose(to[:, tok(c)], pm[:, h, tok(c)], ident)
                    last.then_inc(tile_ps, 1)

                def head_out(h, turned_at):
                    to = tile_bank()
                    pe.wait_ge(tile_out, base + turned_at + 1)
                    pe.matmul(to[:, 0:S], v[:, 0, tok(h)], pT[:, h, 0:S], start=True, stop=False)
                    pe.matmul(to[:, P:S], v[:, 1, tok(h)], pT[:, h, S:S + P], start=False, stop=True).then_inc(tile_ps, 1)

                turned_at = {}
                for h in range(HEADS):
                    turned_at[h] = seen[0]
                    turn(h)
                    if h:
                        head_out(h - 1, turned_at[h - 1])
                head_out(HEADS - 1, turned_at[HEADS - 1])
                assert seen[0] == TILES

                for c in range(KC):
                    w = unit(UNITS - KC + c)
                    pe.wait_ge(tile_out, base + (ZT + 14 + c + 1 if c < 4 else TILES - (0, 5, 3, 1, 0)[c - 3]))
                    for t in range(TT):
                        for b in range(2):
                            last = pe.matmul(yb[2 * t + b][:, :], mixT[:, c, tok(t)], w[:, half(b)], start=c == 0, stop=c == KC - 1)
                            if c == KC - 1:
                                last.then_inc(y_ps, 1)
                    if c < KC - 1:
                        last.then_inc(wout_done, 1)
                    if c == KC - 2:
                        pe.wait_ge(tile_out, base + TILES)
                        gate(l, 1)

            pe.wait_ge(ones_set, 3)
            pe.wait_ge(cst_loaded, 16)
            with pe.Fori(0, DEPTH) as l:
                for m in range(3):
                    modulation(3 * l + m, l, m)
                    transposes(3 * l + m)
                    if m == 1:
                        mixer(l)
                    else:
                        ffn(2 * l + m // 2, lambda: gate(l, m))

            def unit(n):
                slot = n % RING
                pe.wait_ge(unit_loaded[slot], 16 * (-(-(UNITS - slot) // RING) * DEPTH + n // RING + 1))
                return ring[:, slot, :]

            base = TILES * DEPTH
            pe.wait_ge(tables_done, 1)
            pe.wait_ge(gate_done, 6 * DEPTH + 2)
            for r in range(2):
                for u in range(UT):
                    last = pe.transpose(tb[r][:, tok(u)], bbd[:, r, u, :, :, :].rearrange("p j g h -> p (j g h)"), ident)
                last.then_inc(bb_ps, 1)
            transposes(3 * DEPTH)
            pe.wait_ge(hT_ready, 8 * (3 * DEPTH + 1))

            def col_tile(n):
                w, to = unit(n).rearrange("p (c n) -> p c n", c=KC), zb[n % 4]
                if n >= 4:
                    pe.wait_ge(tile_out, base + n - 3)
                elif n >= 2:
                    pe.wait_ge(bb_done, 2)
                for c in range(KC):
                    last = pe.matmul(to[:, 0:S], w[:, c, :], hT[:, c, :], start=c == 0, stop=c == KC - 1)
                last.then_inc(tile_ps, 1)

            def value_tiles():
                w = [unit(12 + c).rearrange("p (c n) -> p c n", c=2) for c in range(4)]
                for t in range(TT):
                    n = 12 + t
                    pe.wait_ge(tile_out, base + n - 3)
                    for c in range(KC):
                        last = pe.matmul(zb[n % 4][:, :], hT[:, c, tok(t)], w[c // 2][:, c % 2, :], start=c == 0, stop=c == KC - 1)
                    last.then_inc(tile_ps, 1)

            def inputs(s):
                u, rows_ = s // 4, slice(32 * (s % 4), 32 * (s % 4) + 32)
                if s >= 2:
                    pe.wait_ge(bu_used, 2 * (s - 1))
                for r in range(2):
                    last = pe.matmul(yb[s % 2][:, S * r:S * (r + 1)], bbT[rows_, r, u, :], u2[rows_, u, :], start=True, stop=True)
                last.then_inc(bu_ps, 1)

            def outputs(s):
                u, rows_ = s // 4, slice(32 * (s % 4), 32 * (s % 4) + 32)
                to = yb[2 + u % 2][rows_, 0:S]
                if s % 4 == 0 and u >= 2:
                    pe.wait_ge(skip_done, u - 1)
                pe.wait_ge(turned, 2 * s + 2)
                for n, (c, rhs) in enumerate(((0, mc[:, s % 2, 0, :]), (1, ms[:, s % 2, 1, :]), (2, mc[:, s % 2, 1, :]), (2, ms[:, s % 2, 0, :]))):
                    last = pe.matmul(to, cz[:, c, s, :, :].rearrange("p g h -> p (g h)"), rhs, start=n == 0, stop=n == 3)
                last.then_inc(c_ps, 1)

            def scores(h):
                if h < 4:
                    pe.wait_ge(tile_out, base + 14)
                    pe.wait_ge(kz_zero, HEADS2)
                else:
                    pe.wait_ge(sm2_done, h - 3)
                for t in range(TT):
                    to = zb[h % 4][:, 0:P] if t == 0 else zb[h % 4][:, P:P + S]
                    last = pe.matmul(to, q2[:, h // 2, tok(t)], kz[:, h, 0:P * (t + 1)], start=True, stop=True)
                last.then_inc(sc2_ps, 1)

            for n in range(4):
                col_tile(n)
            pe.wait_ge(tile_out, base + 4)
            inputs(0)
            inputs(1)
            for s in range(ST):
                if s < 8:
                    col_tile(4 + s)
                elif s == 8:
                    value_tiles()
                else:
                    scores(s - 9)
                outputs(s)
                if s + 2 < ST:
                    inputs(s + 2)
            scores(7)

            def turn2(h):
                if h < 4:
                    pe.wait_ge(sm2_done, h + 5)
                else:
                    pe.wait_ge(pt_out, h - 3)
                pe.wait_ge(p2_done, 2 * h + 2)
                for c in range(3):
                    last = pe.transpose(zb[h % 4][:, tok(c)], pm2[:, h, tok(c)], ident)
                last.then_inc(pt_ps, 1)

            def head_out2(h):
                pe.wait_ge(pt_out, h + 1)
                cols_ = slice(HD2 * h, HD2 * (h + 1))
                pe.matmul(yb[0][:, cols_], pT2[:, h % 4, 0:P], v2[:, 0, cols_], start=True, stop=True)
                pe.matmul(yb[1][:, cols_], pT2[:, h % 4, P:S], v2[:, 0, cols_], start=True, stop=False)
                pe.matmul(yb[1][:, cols_], pT2[:, h % 4, S:S + P], v2[:, 1, cols_], start=False, stop=True).then_inc(o_ps, 1)

            pe.wait_ge(bu_used, 2 * ST)
            for h in range(HEADS2):
                turn2(h)
                if h:
                    head_out2(h - 1)
            head_out2(HEADS2 - 1)

            wg = [unit(16 + c).rearrange("p (c n) -> p c n", c=2) for c in range(2)]
            pe.wait_ge(gelu_done, UT)
            pe.wait_ge(pt_out, HEADS2)
            for e in range(UT):
                for c in range(UT):
                    last = pe.matmul(zb[e][:, 0:S], wg[c // 2][:, c % 2, tok(e)], y2[:, c, :], start=c == 0, stop=c == UT - 1)
                last.then_inc(glu_ps, 1)
            pe.wait_ge(sq2_done, UT)
            pe.wait_ge(skip_done, UT)
            for c in range(UT):
                last = pe.matmul(yb[2][:, 0:S], ones[:, :], sq2[:, c, :], start=c == 0, stop=c == UT - 1)
            last.then_inc(ssm_ss, 1)
            pe.wait_ge(sig_done, UT)
            for t in range(TT):
                pe.wait_ge(on_done, t + 1)
                for c in range(4):
                    last = pe.transpose(tb[c // 2][:, S * (c % 2) + P * t:S * (c % 2) + P * (t + 1)], xn[:, t, 512 + P * c:512 + P * (c + 1)], ident)
                    if t == TT - 1 and c % 2:
                        last.then_inc(ot_ps, 1)
            pe.wait_ge(ssm_rooted, 1)
            pe.wait_ge(o_done, 2)
            for c in range(KC):
                w = unit(UNITS2 - KC + c)
                if c < UT:
                    pe.wait_ge(ssm_done, c + 1)
                else:
                    pe.wait_ge(att_done, c - UT + 1)
                for t in range(TT):
                    for b in range(2):
                        last = pe.matmul(yb[2 * t + b][:, :], mixT2[:, c, tok(t)], w[:, half(b)], start=c == 0, stop=c == KC - 1)
                        if c == KC - 1:
                            last.then_inc(y_ps, 1)
                if c < KC - 1:
                    last.then_inc(wout_done, 1)

            transposes(3 * DEPTH + 1)
            ffn(NFFN - 1, lambda: None)

        @block.scalar
        def _(act):
            step = Steps(act, act_step)
            eps = tiny[:, 0:1]

            def norm(k):
                for t in range(TT):
                    act.wait_ge(x_ready, 4 * k + 2 * t + 2)
                    step.then(act.activation(xn[:, t, :], x[:, t, :], ACT.Square, accum_out=ss[:, t:t + 1]))
                    act.activation(rms[:, t:t + 1], ss[:, t:t + 1], ACT.Sqrt, bias=eps, scale=1.0 / D).then_inc(rms_ready, 1)

            def ffn(f, kt):
                base = FB * f

                def split_gu(n, b, half_n, reused):
                    act.wait_ge(gu_loaded[b], 8 * base + 16 * half_n + 16)
                    if reused:
                        act.wait_ge(gu_ps, base + n - 1)
                    act.activation(gu_hi[:, b, :, :, :].rearrange("p h c n -> p (h c n)"), raw_gu[:, b, :], ACT.Copy).then_inc(gu_hi_done, 1)

                def split_dn(n, b, half_n, reused):
                    act.wait_ge(dn_loaded[b], 8 * base + 16 * half_n + 16)
                    if reused:
                        act.wait_ge(dn_used, (FB - 1) * f + n - 1)
                    act.activation(dn_hi[:, b, :], raw_dn[:, b, :], ACT.Copy).then_inc(dn_hi_done, 1)

                def silu(n, b, reused=True):
                    act.wait_ge(gu_ps, base + n + 1)
                    if reused:
                        act.wait_ge(prod_done, base + n - 1)
                    act.activation(sg[:, b, :], gu_bank[b][:, 0:S], ACT.Silu).then_inc(silu_done, 1)

                split_gu(0, 0, 0, False)
                for j in range(4):
                    act.wait_ge(hT_ready, 8 * kt + 2 * j + 2)
                    act.activation(hT_hi[:, 2 * j:2 * j + 2, :], hT[:, 2 * j:2 * j + 2, :], ACT.Copy).then_inc(hT_hi_done, 1)
                split_dn(0, 0, 0, False)
                split_gu(1, 1, 0, False)
                for b in range(2):
                    silu(b, b, reused=False)
                    split_gu(b + 2, b, 1, True)
                    split_dn(b + 1, 1 - b, b, b == 1)
                with act.Fori(1, FB // 2 - 1) as i:
                    for b in range(2):
                        silu(2 * i + b, b)
                        split_gu(2 * i + b + 2, b, i + 1, True)
                        split_dn(2 * i + b + 1, 1 - b, i + b, True)
                silu(FB - 2, 0)
                split_dn(FB - 1, 1, FB // 2 - 1, True)
                silu(FB - 1, 1)

            def mixer(l):
                base = TILES * l
                seen = [0]

                def take(func, to, width=S, **more):
                    n = seen[0]
                    seen[0] += 1
                    act.wait_ge(tile_ps, base + n + 1)
                    act.activation(to, zb[n % 4][:, 0:width], func, **more).then_inc(tile_out, 1)

                for n in range(7):
                    if n < QCH + KVCH:
                        act.wait_ge(tile_ps, base + n + 1)
                        act.activation(sq[:, n, :], zb[n % 4][:, 0:S], ACT.Square).then_inc(sq_ready, 1)
                    take(ACT.Copy, z[:, n, :])
                for g in range(POOLG):
                    take(ACT.Copy, upad[:, g, PADT:PADT + S])
                    if g == 1:
                        for a, chunks in enumerate((QCH, KVCH)):
                            act.wait_ge(lat_ss, 2 * l + a + 1)
                            act.activation(lat_rms[:, a, :], yb[a][:, 0:S], ACT.Sqrt, bias=eps, scale=1.0 / (P * chunks)).then_inc(lat_rooted, 1)
                for h in range(HEADS):
                    take(ACT.Copy, qn[:, h, :])
                for n in range(4):
                    take(ACT.Copy, qrs[:, n, :])
                for h in range(HEADS):
                    take(ACT.Copy, kn[:, h, :])
                for t in range(TT):
                    take(ACT.Copy, v[:, t, :], 512)
                for g in range(POOLG):
                    take(ACT.Copy, mixT[:, g, :], scale=lc[:, L_PSC + g:L_PSC + g + 1])
                for h in range(HEADS):
                    act.wait_ge(negm_ready, HEADS * l + h + 1)
                    for t, part_ in enumerate((slice(0, P), slice(P, P + S))):
                        act.activation(pm[:, h, part_], pm[:, h, part_], ACT.Exp, bias=negm[:, h, t:t + 1], scale=MLA_SCALE,
                                       accum_out=psum_[:, h, t:t + 1]).then_inc(p_ready, 1)
                for h in range(HEADS):
                    take(ACT.Copy, pT[:, h, :], 384)
                    if h:
                        take(ACT.Copy, mixT[:, POOLG + h - 1, :])
                take(ACT.Copy, mixT[:, POOLG + HEADS - 1, :])
                assert seen[0] == TILES

            act.wait_ge(cst_loaded, 16)
            act.activation(c_act[:, :], cst[:, C_C:C_C + KC], ACT.Silu).then_inc(c_ready, 1)
            act.activation(sp[:, 0, :], cst[:, C_DT:C_DT + ST], ACT.Exp).then_inc(prep_act, 1)
            act.wait_ge(prep_args, 1)
            act.activation(mag[:, :], sp[:, 1, :], ACT.Exp).then_inc(prep_act, 1)
            for to, arg in ((sin1, sp[:, 3, :]), (cos1, sp[:, 4, :]), (sinT, xn[:, 0, 0:S]), (cosT, xn[:, 0, S:2 * S])):
                act.activation(to[:, :], arg, ACT.Sin).then_inc(prep_act, 1)
            act.wait_ge(ones_set, 3)

            with act.Fori(0, DEPTH) as l:
                step.enter_layers(l, ACT_LAYER)
                for m in range(3):
                    norm(3 * l + m)
                    if m == 1:
                        mixer(l)
                    else:
                        ffn(2 * l + m // 2, 3 * l + m)
                step.leave_layers()

            norm(NORMS)
            norm(NORMS + 1)
            for r in range(2):
                act.wait_ge(bb_ps, r + 1)
                act.activation(bbT[:, r, :, :], tb[r][:, :], ACT.Copy).then_inc(bb_done, 1)
            base = TILES * DEPTH
            for n in range(14):
                act.wait_ge(tile_ps, base + n + 1)
                src = zb[n % 4]
                if n < 8:
                    last = act.activation((u2 if n < 4 else q2)[:, n % 4, :], src[:, 0:S], ACT.Copy)
                elif n < 12:
                    for h in (2 * (n - 8), 2 * (n - 8) + 1):
                        rows_ = slice(64 * (h % 2), 64 * (h % 2) + 64)
                        last = act.activation(kz[rows_, h, :], src[rows_, 0:S], ACT.Copy)
                        if h % 2 == 0:
                            step.did(last)
                else:
                    last = act.activation(v2[:, n - 12, :], src[:, :], ACT.Copy)
                last.then_inc(tile_out, 1)
            for h in range(HEADS2):
                act.wait_ge(negm2_done, h + 1)
                for t, part_ in enumerate((slice(0, P), slice(P, P + S))):
                    act.activation(pm2[:, h, part_], pm2[:, h, part_], ACT.Exp, bias=negm2[:, h, t:t + 1], scale=HD2 ** -0.5,
                                   accum_out=psum2[:, t, h:h + 1]).then_inc(p2_done, 1)
            for h in range(HEADS2):
                act.wait_ge(pt_ps, h + 1)
                if h >= 4:
                    act.wait_ge(o_ps, h - 3)
                act.activation(pT2[:, h % 4, :], zb[h % 4][:, 0:384], ACT.Copy).then_inc(pt_out, 1)
            for u in range(UT):
                act.wait_ge(skip_done, u + 1)
                act.activation(y2[:, u, :], y2[:, u, :], ACT.Gelu_apprx_tanh).then_inc(gelu_done, 1)
            for e in range(UT):
                act.wait_ge(glu_ps, e + 1)
                act.activation(sig[:, e, :], zb[e][:, 0:S], ACT.Sigmoid, bias=lc[:, B_GLU + e:B_GLU + e + 1]).then_inc(sig_done, 1)
            for e in range(UT):
                act.wait_ge(glu_done, e + 1)
                act.activation(sq2[:, e, :], sig[:, e, :], ACT.Square).then_inc(sq2_done, 1)
            for t in range(TT):
                act.wait_ge(o_done, t + 1)
                step.then(act.activation(xn[:, t, 512:1024], xn[:, t, 0:512], ACT.Square, accum_out=ss[:, t:t + 1]))
                act.activation(rms[:, t:t + 1], ss[:, t:t + 1], ACT.Sqrt, bias=eps, scale=1.0 / 512).then_inc(o_rooted, 1)
            act.wait_ge(ssm_ss, 1)
            act.activation(rmsT[:, :], yb[2][:, 0:S], ACT.Sqrt, bias=eps, scale=1.0 / 512).then_inc(ssm_rooted, 1)

            def post_norm(done):
                for t in range(TT):
                    for b in range(2):
                        act.wait_ge(y_ps, done + 2 * t + b + 1)
                        step.then(act.activation(xn[:, t, half(b)], yb[2 * t + b][:, :], ACT.Square, accum_out=ss[:, 2 * t + b:2 * t + b + 1]))
                    step.then(act.activation(ss[:, 2 * t:2 * t + 1], ss[:, 2 * t:2 * t + 1], ACT.Identity, bias=eps, scale=1.0 / D))
                    act.activation(rms[:, t:t + 1], ss[:, 2 * t + 1:2 * t + 2], ACT.Sqrt, bias=ss[:, 2 * t:2 * t + 1], scale=1.0 / D).then_inc(post_rooted, 1)

            post_norm(4 * 3 * DEPTH)
            norm(NORMS + 2)
            ffn(NFFN - 1, 3 * DEPTH + 1)
            post_norm(4 * (3 * DEPTH + 1))

        @block.vector
        def _(dve):
            step = Steps(dve, dve_step)

            def turn_into(r, r_cos, angle, tmp):
                pi = 3.1415925
                step.then(dve.tensor_scalar(tmp, angle, 1 / TWO_PI, ROUND, ALU.mult, ALU.add))
                step.then(dve.tensor_scalar(tmp, tmp, -ROUND, None, ALU.add))
                for n, piece in enumerate(split_two_pi(4, 9)):
                    step.then(dve.scalar_tensor_tensor(r, tmp, -piece, r if n else angle, ALU.mult, ALU.add))
                step.then(dve.tensor_scalar(r, r, pi, -pi, ALU.min, ALU.max))
                step.then(dve.tensor_scalar(tmp, r, math.pi / 2, -TWO_PI, ALU.is_gt, ALU.mult))
                step.then(dve.scalar_tensor_tensor(r_cos, r, math.pi / 2, tmp, ALU.add, ALU.add))
                return dve.tensor_scalar(r_cos, r_cos, pi, -pi, ALU.min, ALU.max)

            def modulation(k, l, m):
                dve.wait_ge(lc_loaded, 16 * l + 16)
                dve.wait_ge(mod_ps, k + 1)
                step.then(dve.tensor_tensor(mods[:, :], tb[0][:, 0:16], lc[:, L_ADA + 16 * m:L_ADA + 16 * m + 16], ALU.add))
                dve.scalar_tensor_tensor(gs[:, :], mods[:, KC:2 * KC], 1.0, lc[:, L_NORM + KC * m:L_NORM + KC * m + KC], ALU.add, ALU.mult)\
                   .then_inc(mod_done, 1)

            def norm(k):
                for t in range(TT):
                    dve.wait_ge(rms_ready, 2 * k + t + 1)
                    step.then(dve.reciprocal(rstd[:, t:t + 1], rms[:, t:t + 1]))
                    dve.tensor_scalar(xn[:, t, :], x[:, t, :], rstd[:, t:t + 1], None, ALU.mult).then_inc(xn_ready, 1)

            def modulated(kt, gain, shift=None):
                for c in range(KC):
                    if c % 2 == 0:
                        dve.wait_ge(tr_ready, 4 * kt + c // 2 + 1)
                    src = yb[c // 2][:, S * (c % 2):S * (c % 2 + 1)]
                    if shift is None:
                        dve.tensor_scalar(hT[:, c, :], src, gain[:, c:c + 1], None, ALU.mult).then_inc(hT_ready, 1)
                    else:
                        dve.tensor_scalar(hT[:, c, :], src, gain[:, c:c + 1], shift[:, c:c + 1], ALU.mult, ALU.add).then_inc(hT_ready, 1)

            def ffn(f, modulate):
                base = FB * f

                def split_gu(n, b):
                    dve.wait_ge(gu_hi_done, base + n + 1)
                    dve.tensor_tensor(gu_lo[:, b, :, :, :].rearrange("p h c n -> p (h c n)"), raw_gu[:, b, :],
                                      gu_hi[:, b, :, :, :].rearrange("p h c n -> p (h c n)").bitcast(F32), ALU.subtract).then_inc(gu_lo_done, 1)

                def split_dn(n, b):
                    dve.wait_ge(dn_hi_done, base + n + 1)
                    dve.tensor_tensor(dn_lo[:, b, :], raw_dn[:, b, :], dn_hi[:, b, :].bitcast(F32), ALU.subtract).then_inc(dn_lo_done, 1)

                def hidden(n, b, reused=True):
                    dve.wait_ge(silu_done, base + n + 1)
                    dve.tensor_tensor(prod[:, b, :], sg[:, b, :], gu_bank[b][:, S:2 * S], ALU.mult).then_inc(prod_done, 1)
                    if reused:
                        dve.wait_ge(dn_used, (FB - 1) * f + n - 1)
                    dve.wait_ge(prod_done, base + n + 1)
                    dve.tensor_copy(act_hi[:, b, :], prod[:, b, :]).then_inc(act_hi_done, 1)
                    dve.wait_ge(act_hi_done, base + n + 1)
                    dve.tensor_tensor(act_lo[:, b, :], prod[:, b, :], act_hi[:, b, :].bitcast(F32), ALU.subtract).then_inc(act_done, 1)

                split_gu(0, 0)
                modulate()
                for j in range(4):
                    dve.wait_ge(hT_hi_done, 4 * f + j + 1)
                    dve.tensor_tensor(hT_lo[:, 2 * j:2 * j + 2, :], hT[:, 2 * j:2 * j + 2, :], hT_hi[:, 2 * j:2 * j + 2, :].bitcast(F32),
                                      ALU.subtract).then_inc(hT_lo_done, 1)
                split_dn(0, 0)
                split_gu(1, 1)
                for b in range(2):
                    hidden(b, b, reused=False)
                    split_gu(b + 2, b)
                    split_dn(b + 1, 1 - b)
                with dve.Fori(1, FB // 2 - 1) as i:
                    for b in range(2):
                        hidden(2 * i + b, b)
                        split_gu(2 * i + b + 2, b)
                        split_dn(2 * i + b + 1, 1 - b)
                hidden(FB - 2, 0)
                split_dn(FB - 1, 1)
                hidden(FB - 1, 1)

            def residual(k, scale):
                for b in range(2):
                    dve.wait_ge(gbias_loaded, 16 * k + 16)
                    dve.wait_ge(gate_ps, 2 * k + b + 1)
                    dve.tensor_tensor(gate_b[:, half(b)], gate_b[:, half(b)], tb[b][:, :], ALU.add).then_inc(gate_done, 1)
                dve.wait_ge(gate_done, 2 * k + 4)
                for t in range(TT):
                    for b in range(2):
                        dve.wait_ge(y_ps, 4 * k + 2 * t + b + 1)
                        step.did(dve.scalar_tensor_tensor(xn[:, t, half(b)], yb[2 * t + b][:, :], scale, gate_b[:, half(b)], ALU.mult, ALU.mult))
                    step.settle()
                    for b in range(2):
                        dve.tensor_tensor(x[:, t, half(b)], x[:, t, half(b)], xn[:, t, half(b)], ALU.add).then_inc(x_ready, 1)

            def rope(to, straight, swapped, heads, scratch):
                wide = [P, heads, S]
                step.did(dve.tensor_tensor(scratch[:, 0, 0:heads, :], straight, cosT[:, :].unsqueeze(1).to_broadcast(wide), ALU.mult))
                step.then(dve.tensor_tensor(scratch[:, 1, 0:heads, :], swapped, sinT[:, :].unsqueeze(1).to_broadcast(wide), ALU.mult))
                for rows_, dst in to:
                    last = dve.tensor_tensor(dst, scratch[rows_, 0, 0:heads, :], scratch[rows_, 1, 0:heads, :], ALU.add)
                    yield last

            def mixer(l):
                base = TILES * l
                for a, (first, count, at) in enumerate(((0, QCH, L_QN), (QCH, KVCH, L_KVN))):
                    dve.wait_ge(lat_rooted, 2 * l + a + 1)
                    step.then(dve.reciprocal(lat_rms[:, a, :], lat_rms[:, a, :]))
                    for c in range(count):
                        dve.scalar_tensor_tensor(latn[:, first + c, :], z[:, first + c, :], lc[:, at + c:at + c + 1], lat_rms[:, a, :],
                                                 ALU.mult, ALU.mult).then_inc(lat_done, 1)
                dve.wait_ge(tile_out, base + 7)
                step.did(dve.memset(krz[64:128, 0, :], 0.0))
                step.did(dve.memset(krz[0:64, 1, :], 0.0))
                for last in rope([(slice(0, 64), krz[0:64, 0:1, :]), (slice(64, 128), krz[64:128, 1:2, :])], z[:, 5:6, :], z[:, 6:7, :], 1, rot):
                    last.then_inc(kr_ready, 1)
                step.did(dve.memset(upad[:, :, 0:PADT], 0.0))
                dve.wait_ge(tile_out, base + ZT)
                step.settle()
                end = PADT + S
                step.then(dve.tensor_tensor(sumA[:, :, 1:end], upad[:, :, 1:end], upad[:, :, 0:end - 1], ALU.add))
                step.then(dve.tensor_tensor(sumB[:, :, 3:end], sumA[:, 1:4, 3:end], sumA[:, 1:4, 1:end - 2], ALU.add))
                step.then(dve.tensor_tensor(sumA[:, 2:4, 7:end], sumB[:, 1:3, 7:end], sumB[:, 1:3, 3:end - 4], ALU.add))
                step.then(dve.tensor_tensor(sumB[:, 2, 15:end], sumA[:, 3, 15:end], sumA[:, 3, 7:end - 8], ALU.add))
                sums = (sumA[:, 0], sumB[:, 0], sumA[:, 2], sumB[:, 2])
                for g, s in enumerate(sums):
                    ratio = cst[:, C_RATIO + PADT * g:C_RATIO + PADT * (g + 1)]
                    step.did(dve.tensor_tensor(s[:, PADT:2 * PADT], s[:, PADT:2 * PADT], ratio, ALU.mult))
                step.settle()
                for g, s in enumerate(sums):
                    dve.scalar_tensor_tensor(s[:, PADT:end], s[:, PADT:end], 0.5 ** (g + 1), upad[:, g, PADT:end], ALU.mult, ALU.subtract)\
                       .then_inc(diff_ready, 1)
                dve.wait_ge(tile_out, base + ZT + 8)
                dve.wait_ge(kr_ready, 2 * l + 2)
                for last in rope([(slice(0, P), qr[:, :, :])], qrs[:, 0:2, :], qrs[:, 2:4, :], 2, rot):
                    last.then_inc(qr_ready, 1)
                for h in range(HEADS):
                    dve.wait_ge(sc_ps, HEADS * l + h + 1)
                    step.then(dve.tensor_tensor(pm[:, h, :], yb[h][:, 0:384], mask, ALU.add))
                    step.did(dve.reduce_max(rmax[:, h, 0:1], pm[:, h, 0:P], axis=AX.X))
                    step.then(dve.reduce_max(rmax[:, h, 1:2], pm[:, h, P:P + S], axis=AX.X))
                    dve.tensor_scalar(negm[:, h, :], rmax[:, h, :], -MLA_SCALE, None, ALU.mult).then_inc(negm_ready, 1)
                for h in range(HEADS):
                    dve.wait_ge(p_ready, 2 * (HEADS * l + h + 1))
                    step.then(dve.reciprocal(prec[:, h, :], psum_[:, h, :]))
                    for t, part_ in enumerate((slice(0, P), slice(P, P + S))):
                        dve.tensor_scalar(pm[:, h, part_], pm[:, h, part_], prec[:, h, t:t + 1], None, ALU.mult).then_inc(pn_ready, 1)

            dve.wait_ge(cst_loaded, 16)
            a_re, a_im = cst[:, C_ARE:C_ARE + ST], cst[:, C_AIM:C_AIM + ST]
            dve.wait_ge(prep_act, 1)
            step.did(dve.tensor_tensor(sp[:, 1, :], a_re, sp[:, 0, :], ALU.mult))
            step.then(dve.tensor_tensor(sp[:, 2, :], a_im, sp[:, 0, :], ALU.mult))
            step.did(turn_into(sp[:, 3, :], sp[:, 4, :], sp[:, 2, :], sp[:, 5, :]))
            dve.wait_ge(pos_loaded, 16)
            step.then(dve.tensor_copy(xn[:, 1, S:2 * S], pos_i))
            step.then(dve.tensor_scalar(xn[:, 0, 2 * S:3 * S], xn[:, 1, S:2 * S], cst[:, C_FREQ:C_FREQ + 1], None, ALU.mult))
            turn_into(xn[:, 0, 0:S], xn[:, 0, S:2 * S], xn[:, 0, 2 * S:3 * S], xn[:, 1, 2 * S:3 * S]).then_inc(prep_args, 1)
            dve.wait_ge(prep_act, 6)
            nr, li, den = sp[:, 0, :], sp[:, 1, :], sp[:, 2, :]
            step.did(dve.tensor_tensor(nr, mag[:, :], cos1[:, :], ALU.mult))
            step.did(dve.tensor_tensor(li, mag[:, :], sin1[:, :], ALU.mult))
            step.did(dve.tensor_tensor(den, a_re, a_re, ALU.mult))
            step.did(dve.tensor_tensor(sp[:, 3, :], a_im, a_im, ALU.mult))
            step.then(dve.tensor_scalar(sinT[:, :], sinT[:, :], cst[:, C_SIGN:C_SIGN + 1], None, ALU.mult))
            step.did(dve.tensor_scalar(nr, nr, -1.0, None, ALU.add))
            step.then(dve.tensor_tensor(den, den, sp[:, 3, :], ALU.add))
            step.did(dve.reciprocal(den, den))
            step.did(dve.tensor_tensor(sp[:, 3, :], nr, a_re, ALU.mult))
            step.did(dve.tensor_tensor(sp[:, 4, :], li, a_im, ALU.mult))
            step.did(dve.tensor_tensor(sp[:, 5, :], li, a_re, ALU.mult))
            step.then(dve.tensor_tensor(sp[:, 6, :], nr, a_im, ALU.mult))
            step.did(dve.tensor_tensor(sp[:, 3, :], sp[:, 3, :], sp[:, 4, :], ALU.add))
            step.then(dve.tensor_tensor(sp[:, 5, :], sp[:, 5, :], sp[:, 6, :], ALU.subtract))
            step.did(dve.tensor_tensor(cre[:, :], sp[:, 3, :], den, ALU.mult))
            dve.tensor_tensor(cim[:, :], sp[:, 5, :], den, ALU.mult).then_inc(prep_dve, 1)

            dve.wait_ge(c_ready, 1)
            at = {}
            for n in range(0, 6, 2):
                for c in range(KC):
                    for m in (n, n + 1):
                        to = part[:, m // 4, S * (m % 4):S * (m % 4 + 1)]
                        if c == 0:
                            dve.wait_ge(pro_loaded[m], 16)
                            step.did(dve.tensor_scalar(to, pro[:, m, 0, :], c_act[:, 0:1], None, ALU.mult))
                            at[m] = step.n
                            continue
                        dve.wait_ge(dve_step, at[m])
                        last = dve.scalar_tensor_tensor(to, pro[:, m, c, :], c_act[:, c:c + 1], to, ALU.mult, ALU.add)
                        if c < KC - 1:
                            step.did(last)
                            at[m] = step.n
                        else:
                            last.then_inc(pro_done, 1)
            dve.wait_ge(x_loaded, 16)
            dve.sem_inc(x_ready, 4)
            dve.sem_inc(gate_done, 2)

            with dve.Fori(0, DEPTH) as l:
                step.enter_layers(l, DVE_LAYER)
                for m in range(3):
                    k = 3 * l + m
                    modulation(k, l, m)
                    norm(k)
                    if m == 1:
                        modulated(k, gs, mods)
                        mixer(l)
                    else:
                        ffn(2 * l + m // 2, lambda: modulated(k, gs, mods))
                    residual(k, 1.0 if m == 1 else 0.5)
                step.leave_layers()

            dve.wait_ge(final_loaded, 16)
            for t in range(TT):
                dve.wait_ge(rms_ready, 2 * NORMS + t + 1)
                step.then(dve.reciprocal(rstd[:, t:t + 1], rms[:, t:t + 1]))
                dve.scalar_tensor_tensor(x[:, t, :], x[:, t, :], rstd[:, t:t + 1], final_b[:, :], ALU.mult, ALU.mult).then_inc(x_ready, 2)

            def skip(u):
                dve.wait_ge(c_ps, 4 * u + 4)
                dve.scalar_tensor_tensor(y2[:, u, :], u2[:, u, :], lc[:, B_SKIP + u:B_SKIP + u + 1], yb[2 + u % 2][:, 0:S],
                                         ALU.mult, ALU.add).then_inc(skip_done, 1)

            def masked(h):
                dve.wait_ge(sc2_ps, h + 1)
                dve.tensor_tensor(pm2[:, h, :], zb[h % 4][:, 0:384], mask, ALU.add).then_inc(sm2_done, 1)
                dve.wait_ge(sm2_done, h + 1)
                step.did(dve.reduce_max(rmax2[:, h, 0:1], pm2[:, h, 0:P], axis=AX.X))
                step.then(dve.reduce_max(rmax2[:, h, 1:2], pm2[:, h, P:P + S], axis=AX.X))
                dve.tensor_scalar(negm2[:, h, :], rmax2[:, h, :], -HD2 ** -0.5, None, ALU.mult).then_inc(negm2_done, 1)

            dve.wait_ge(lc_loaded, 16 * DEPTH + 16)
            norm(NORMS + 1)
            modulated(3 * DEPTH, lc[:, B_MIX:B_MIX + KC])
            for s in range(ST):
                dve.wait_ge(bu_ps, s + 1)
                bu = yb[s % 2][:, :].rearrange("p (r n) -> p r n", r=2)
                for to, table in ((ma, ecos), (mb, esin)):
                    dve.tensor_tensor(to[:, :, :], bu, table[:, s, :].unsqueeze(1).to_broadcast([P, 2, S]), ALU.mult).then_inc(bu_used, 1)
                dve.wait_ge(bu_used, 2 * s + 2)
                step.did(dve.tensor_tensor(vin[:, 0, :], ma[:, 0, :], mb[:, 1, :], ALU.add))
                step.then(dve.tensor_tensor(vin[:, 1, :], ma[:, 1, :], mb[:, 0, :], ALU.subtract))
                if s >= 3:
                    dve.wait_ge(turned, 2 * (s - 2))
                for r in range(2):
                    last = dve.tensor_tensor_scan(ysc[:, s % 3, r, :], mag[:, s:s + 1].to_broadcast([P, S]), vin[:, r, :], 0.0, ALU.mult, ALU.add)
                    if r == 0:
                        step.did(last)
                last.then_inc(scanned, 1)
                if s % 4 == 1 and s > 4:
                    skip(s // 4 - 1)
                if s >= 10:
                    masked(s - 10)
            for h in range(6, HEADS2):
                masked(h)
            skip(UT - 1)
            dve.wait_ge(p2_done, 2 * HEADS2)
            step.then(dve.reciprocal(prec2[:, :, :], psum2[:, :, :]))
            dve.wait_ge(o_ps, HEADS2)
            for t in range(TT):
                dve.tensor_tensor(xn[:, t, 0:512].rearrange("p (h n) -> p h n", n=HD2), yb[t][:, :].rearrange("p (h n) -> p h n", n=HD2),
                                  prec2[:, t, :].unsqueeze(2).to_broadcast([P, HEADS2, HD2]), ALU.mult).then_inc(o_done, 1)
            for e in range(UT):
                dve.wait_ge(sig_done, e + 1)
                dve.tensor_tensor(sig[:, e, :], sig[:, e, :], y2[:, e, :], ALU.mult).then_inc(glu_done, 1)
            for t in range(TT):
                dve.wait_ge(o_rooted, t + 1)
                step.then(dve.reciprocal(rstd[:, t:t + 1], rms[:, t:t + 1]))
                dve.tensor_scalar(xn[:, t, 512:1024], xn[:, t, 0:512], rstd[:, t:t + 1], None, ALU.mult).then_inc(on_done, 1)
            dve.wait_ge(ssm_rooted, 1)
            step.then(dve.reciprocal(rstdT[:, :], rmsT[:, :]))
            for c in range(UT):
                dve.scalar_tensor_tensor(mixT2[:, c, :], sig[:, c, :], lc[:, B_SSM + c:B_SSM + c + 1], rstdT[:, :], ALU.mult, ALU.mult).then_inc(ssm_done, 1)
            for c in range(UT):
                dve.wait_ge(ot_ps, c // 2 + 1)
                dve.tensor_scalar(mixT2[:, UT + c, :], tb[c // 2][:, S * (c % 2):S * (c % 2 + 1)], lc[:, B_ATT + c:B_ATT + c + 1], None, ALU.mult)\
                   .then_inc(att_done, 1)

            def post_norm(n, row):
                for t in range(TT):
                    dve.wait_ge(post_rooted, 2 * n + t + 1)
                    step.then(dve.reciprocal(rstd[:, t:t + 1], rms[:, t:t + 1]))
                    for b in range(2):
                        step.did(dve.scalar_tensor_tensor(xn[:, t, half(b)], yb[2 * t + b][:, :], rstd[:, t:t + 1], row[:, half(b)], ALU.mult, ALU.mult))
                    step.settle()
                    for b in range(2):
                        dve.tensor_tensor(x[:, t, half(b)], x[:, t, half(b)], xn[:, t, half(b)], ALU.add).then_inc(x_ready, 1)

            dve.wait_ge(row_loaded, 16)
            post_norm(0, row_b)
            norm(NORMS + 2)
            ffn(NFFN - 1, lambda: modulated(3 * DEPTH + 1, lc[:, B_FFN:B_FFN + KC]))
            dve.wait_ge(gbias_loaded, 16 * 3 * DEPTH + 16)
            post_norm(1, gate_b)


def tiles_of(w):
    return w.reshape(KC, P, -1, P).transpose(2, 1, 0, 3)


def columns(v):
    return np.asarray(v).reshape(-1, P).T


def kernel(**inputs):
    import concourse.bacc as bacc
    from concourse.bass_utils import run_bass_kernel_spmd

    a = {k: np.asarray(v) for k, v in inputs.items()}
    f32 = np.float32

    def ffn_weights(kind):
        first = [a[f"ffn{n}_w_{kind}"][l] for l in range(DEPTH) for n in (1, 2)]
        return [*first, a[f"w_{kind}_2"][0]]

    gu = np.empty((NFFN, FB, P, 2, KC, P), f32)
    dn = np.empty((NFFN, FB, P, D), f32)
    for f, (g, u, d) in enumerate(zip(*map(ffn_weights, ("gate", "up", "down")))):
        gu[f, :, :, 0], gu[f, :, :, 1], dn[f] = tiles_of(g), tiles_of(u), d.reshape(FB, P, D)

    ada = a["ada_w"].reshape(DEPTH, KC, P, 36, S).transpose(0, 3, 2, 1, 4).reshape(DEPTH * 36, P, KC * S)

    kr = np.arange(1152, 1216)
    z_cols = np.concatenate([np.arange(512, 1152), kr, kr, np.roll(kr, 32), np.roll(kr, 32), np.arange(512)])
    q_cols = np.arange(HEADS * 192).reshape(HEADS, 192)
    rope = q_cols[:, 128:]
    q_cols = np.concatenate([q_cols[:, :128].ravel(), rope.ravel(), np.roll(rope, 32, 1).ravel()])
    kv_cols = np.arange(HEADS * 256).reshape(HEADS, 2, P).transpose(1, 0, 2).ravel()
    mix = np.zeros((DEPTH, UNITS, P, D), f32)
    for l in range(DEPTH):
        mix[l, :ZT] = tiles_of(a["w_in"][l][:, z_cols]).reshape(ZT, P, D)
        mix[l, ZT:ZT + QCH] = a["w_q_b"][l][:, q_cols].reshape(QCH, P, D)
        mix[l, ZT + QCH:ZT + QCH + KVCH] = a["w_kv_b"][l][:, kv_cols].reshape(KVCH, P, D)
        mix[l, ZT + QCH + KVCH, :, :512] = a["pool_w"][l].transpose(1, 0, 2).reshape(P, 512)
        mix[l, UNITS - KC:] = a["w_out"][l].reshape(KC, P, D)
    mix = mix.reshape(DEPTH * UNITS, P, D)
    w_in = a["w_in_2"][0]
    mix2 = np.empty((UNITS2, P, D), f32)
    mix2[:12] = tiles_of(w_in[:, :1536]).reshape(12, P, D)
    mix2[12:16] = w_in[:, 1536:].reshape(4, 2, P, 512).transpose(0, 2, 1, 3).reshape(4, P, D)
    mix2[16:18] = a["w_glu_2"][0].reshape(2, 2, P, 512).transpose(0, 2, 1, 3).reshape(2, P, D)
    mix2[18:] = a["w_out_2"][0].reshape(KC, P, D)

    consts = np.zeros((P, C_N), f32)
    consts[:, C_C:C_C + KC] = columns(a["c"][0])
    consts[:, C_FREQ] = np.tile((1.0 / (f32(10000.0) ** (np.arange(0, 64, 2, dtype=f32) / f32(64)))).astype(f32), 4)
    consts[:, C_SIGN] = np.tile(np.repeat([-1.0, 1.0], 32), 2)
    consts[:, C_ARE:C_ARE + ST] = columns(a["ssm_a_re_2"][0])
    consts[:, C_AIM:C_AIM + ST] = columns(a["ssm_a_im_2"][0])
    consts[:, C_DT:C_DT + ST] = columns(np.repeat(a["ssm_log_dt_2"][0], 64))
    for g in range(POOLG):
        w = 2 ** (g + 1)
        consts[:, C_RATIO + PADT * g:C_RATIO + PADT * (g + 1)] = w / np.minimum(np.arange(PADT) + 1, w)
    tri = np.where(np.arange(P)[:, None] >= np.arange(P)[None, :], 0.0, MASKED)
    consts[:, C_MASK:C_MASK + P] = consts[:, C_MASK + S:C_MASK + S + P] = tri
    consts[:, C_ID:C_ID + P] = np.eye(P)
    for at, name, order in ((C_BRE, "ssm_b_re_2", None), (C_BIM, "ssm_b_im_2", None), (C_CRE, "ssm_c_re_2", 1), (C_CIM, "ssm_c_im_2", 1)):
        w = a[name][0].transpose(0, 2, 1) if order else a[name][0]
        consts[:, at:at + 256] = w.reshape(ST, P, 16).transpose(1, 0, 2).reshape(P, 256)

    cols = np.zeros((DEPTH + 1, P, L_N), f32)
    gate_rows = np.empty((3 * DEPTH, D), f32)
    for l in range(DEPTH):
        b = a["ada_b"][l].reshape(3, 3, D)
        for m in range(3):
            cols[l, :, L_ADA + 16 * m:L_ADA + 16 * m + 16] = columns(b[m, :2])
            gate_rows[3 * l + m] = b[m, 2]
        for m, name in enumerate(("ffn1_norm", "mix_norm", "ffn2_norm")):
            cols[l, :, L_NORM + KC * m:L_NORM + KC * (m + 1)] = columns(a[name][l])
        cols[l, :, L_PSC:L_PSC + 4] = columns(a["pool_scale"][l])
        cols[l, :, L_QN:L_QN + QCH] = columns(a["q_a_norm"][l])
        cols[l, :, L_KVN:L_KVN + KVCH] = columns(a["kv_a_norm"][l])
    for at, name in ((B_MIX, "g_pre_mix_2"), (B_FFN, "g_pre_ffn_2"), (B_SSM, "g_ssm_out_2"), (B_ATT, "g_attn_out_2"), (B_GLU, "b_glu_2"), (B_SKIP, "ssm_d_2")):
        got = columns(a[name][0])
        cols[DEPTH, :, at:at + got.shape[1]] = got
    rows = np.stack([a["final_norm"], a["g_post_mix_2"][0], a["g_post_ffn_2"][0]])

    nc = bacc.Bacc("TRN2", target_bir_lowering=False, num_devices=1)
    arrays = {
        "x_in": a["x"][0], "positions": a["positions"], "consts": consts, "cols": cols, "gate_rows": gate_rows, "rows": rows, "ada": ada,
        "ffn_gu": gu.reshape(NFFN * FB, P, 2 * KC * P), "ffn_dn": dn.reshape(NFFN * FB, P, D), "mix_w": mix, "mix2_w": mix2,
    }
    arrays = {k: np.ascontiguousarray(v) for k, v in arrays.items()}
    aps = [nc.dram_tensor(k, v.shape, mybir.dt.from_np(v.dtype), kind="ExternalInput").ap() for k, v in arrays.items()]
    out = nc.dram_tensor("x_out", (S, D), F32, kind="ExternalOutput").ap()
    program(nc, *aps, out)
    r = run_bass_kernel_spmd(nc, [arrays], core_ids=[0])
    return r.results[0]["x_out"].reshape(1, S, D)
```

```python
import math
from contextlib import ExitStack

import numpy as np

import concourse.bass as bass
from concourse import mybir

F32 = mybir.dt.float32
F32R = mybir.dt.float32r
I32 = mybir.dt.int32
ALU = mybir.AluOpType
ACT = mybir.ActivationFunctionType
AX = mybir.AxisListType

P = 128
D = 1024
S = 256
TT = S // P
KC = D // P
FF = 2816
FB = FF // P
DEPTH = 2
NFFN = 2 * DEPTH + 1
EPS = 1e-6

HEADS = 4
POOLG = 4
QCH, KVCH = 3, 2
MLA_SCALE = 1.0 / math.sqrt(192)
ZT = 11
TILES = 37
UNITS = 25
POOL_UNIT = 15
SPLITS = UNITS - 1
PADT = 16

HEADS2, HD2 = 8, 64
ST = 16
UT = 4
UNITS2 = 24

RING = 3
SLOTS = 3
MASKED = -1e30
TWO_PI = 2 * math.pi
ROUND = 12582912.0

C_C, C_FREQ, C_SIGN, C_ARE, C_AIM, C_DT, C_ID = 0, 8, 9, 10, 26, 42, 58
C_RATIO = C_ID + P
C_MASK = C_RATIO + 4 * PADT
C_BRE = C_MASK + 384
C_BIM, C_CRE, C_CIM = C_BRE + 256, C_BRE + 512, C_BRE + 768
C_N = C_BRE + 1024
L_ADA, L_NORM, L_PSC, L_QN, L_KVN, L_N = 0, 48, 72, 76, 79, 81
B_MIX, B_FFN, B_SSM, B_ATT, B_GLU, B_SKIP = 0, 8, 16, 20, 24, 28


def split_two_pi(parts, bits):
    rest, out = TWO_PI, []
    for n in range(parts):
        if n == parts - 1:
            out.append(float(np.float32(rest)))
        else:
            scale = 2.0 ** (bits - 1 - math.floor(math.log2(rest)))
            out.append(math.floor(rest * scale) / scale)
        rest -= out[-1]
    return out


class Steps:

    def __init__(self, engine, sem):
        self.engine, self.sem, self.base, self.n = engine, sem, 0, 0

    def did(self, instruction):
        instruction.then_inc(self.sem, 1)
        self.n += 1

    def settle(self):
        self.engine.wait_ge(self.sem, self.base + self.n)

    def then(self, instruction):
        self.did(instruction)
        self.settle()

    def enter_layers(self, layer, per_layer):
        self.before = self.base + self.n
        self.base, self.n, self.per_layer = self.before + layer * per_layer, 0, per_layer

    def leave_layers(self):
        assert self.n == self.per_layer, (self.n, self.per_layer)
        self.base, self.n = self.before + DEPTH * self.per_layer, 0


DVE_LAYER = 57
ACT_LAYER = 34


def program(nc, x_in, positions, consts, cols, gate_rows, rows, ada, ffn_gu, ffn_dn, mix_w, mix2_w, out):
    ctx = ExitStack()
    with ctx:
        def sem(name):
            return ctx.enter_context(nc.semaphore(name))

        def bank(name):
            return ctx.enter_context(nc.psum_tensor(name, [P, 512], F32))

        def sb(stack, name, shape, dt=F32):
            return stack.enter_context(nc.sbuf_tensor(name, shape, dt))

        x = sb(ctx, "x", [P, TT, D])
        xn = sb(ctx, "xn", [P, TT, D])
        hT = sb(ctx, "hT", [P, KC, S])
        hT_hi = sb(ctx, "hT_hi", [P, KC, S], F32R)
        hT_lo = sb(ctx, "hT_lo", [P, KC, S], F32R)
        raw_gu = sb(ctx, "raw_gu", [P, 2, 2 * KC * P])
        raw_dn = sb(ctx, "raw_dn", [P, 2, D])
        dn_hi = sb(ctx, "dn_hi", [P, SLOTS, D], F32R)
        dn_lo = sb(ctx, "dn_lo", [P, SLOTS, D], F32R)
        ring = sb(ctx, "ring", [P, RING, D])
        gate_b = sb(ctx, "gate_b", [P, D])
        cst = sb(ctx, "cst", [P, C_N])
        lc = sb(ctx, "lc", [P, L_N])
        cosT = sb(ctx, "cosT", [P, S])
        sinT = sb(ctx, "sinT", [P, S])
        ones = sb(ctx, "ones", [P, P])
        tiny = sb(ctx, "tiny", [P, 2])
        c_act = sb(ctx, "c_act", [P, KC])
        mods = sb(ctx, "mods", [P, 16])
        gs = sb(ctx, "gs", [P, KC])
        ss = sb(ctx, "ss", [P, 4])
        rms = sb(ctx, "rms", [P, 2])
        rstd = sb(ctx, "rstd", [P, 2])
        junk = sb(ctx, "junk", [P, 1])
        mag = sb(ctx, "mag", [P, ST])
        cos1 = sb(ctx, "cos1", [P, ST])
        sin1 = sb(ctx, "sin1", [P, ST])
        cre = sb(ctx, "cre", [P, ST])
        cim = sb(ctx, "cim", [P, ST])
        cz = sb(ctx, "cz", [P, 2, ST, 2, 16])
        sp = sb(ctx, "sp", [P, 8, ST])
        ident = cst[:, C_ID:C_ID + P]
        mask = cst[:, C_MASK:C_MASK + 384]

        area = ExitStack()
        ada_in = sb(area, "ada_in", [P, 2, KC, S])
        part = sb(area, "part", [P, 7, D])
        area.close()
        ecos = sb(ctx, "ecos", [P, ST, S])
        esin = sb(ctx, "esin", [P, ST, S])
        bbd = sb(ctx, "bbd", [P, 2, UT, 4, 2, 16])
        row_b = sb(ctx, "row_b", [P, D])
        ma = sb(ctx, "ma", [P, 2, S])
        area = ExitStack()
        mb = sb(area, "mb", [P, 2, S])
        area.close()
        rmsT = sb(ctx, "rmsT", [P, S])
        rstdT = sb(ctx, "rstdT", [P, S])
        work = ExitStack()
        pro = sb(work, "pro", [P, 5, KC, S])
        work.close()
        work = ExitStack()
        gu_hi = sb(work, "gu_hi", [P, 2, 2, KC, P], F32R)
        gu_lo = sb(work, "gu_lo", [P, 2, 2, KC, P], F32R)
        sg = sb(work, "sg", [P, 2, S])
        prod = sb(work, "prod", [P, 2, S])
        act_hi = sb(work, "act_hi", [P, 2, S], F32R)
        act_lo = sb(work, "act_lo", [P, 2, S], F32R)
        work.close()
        work = ExitStack()
        lat = ExitStack()
        z = sb(lat, "z", [P, 7, S])
        lat.close()
        qrs = sb(work, "qrs", [P, 4, S])
        sb(work, "z_end", [P, 3, S])
        lat = ExitStack()
        sq = sb(lat, "sq", [P, QCH + KVCH, S])
        lat.close()
        lat = ExitStack()
        lat_hi = sb(lat, "lat_hi", [P, QCH + KVCH, S], F32R)
        lat_lo = sb(lat, "lat_lo", [P, QCH + KVCH, S], F32R)
        lat.close()
        pm = sb(work, "pm", [P, HEADS, 384])
        sb(work, "lat_end", [P, 2 * (QCH + KVCH) * S - HEADS * 384])
        qn = sb(work, "qn", [P, HEADS, S])
        qr = sb(work, "qr", [P, 2, S])
        krz = sb(work, "krz", [P, 2, S])
        lat = ExitStack()
        lat_rms = sb(lat, "lat_rms", [P, 2, S])
        lat.close()
        kn = sb(work, "kn", [P, HEADS, S])
        pools = ExitStack()
        upad = sb(pools, "upad", [P, POOLG, PADT + S])
        sumA = sb(pools, "sumA", [P, POOLG, PADT + S])
        sumB = sb(pools, "sumB", [P, POOLG - 1, PADT + S])
        pools.close()
        pT = sb(work, "pT", [P, HEADS, 384])
        v = sb(work, "v", [P, TT, HEADS * P])
        sb(work, "pools_end", [P, (3 * POOLG - 1) * (PADT + S) - HEADS * 384 - TT * HEADS * P])
        rot = sb(work, "rot", [P, 2, 2, S])
        rmax = sb(work, "rmax", [P, HEADS, 2])
        negm = sb(work, "negm", [P, HEADS, 2])
        psum_ = sb(work, "psums", [P, HEADS, 2])
        prec = sb(work, "prec", [P, HEADS, 2])
        work.close()
        work = ExitStack()
        u2 = sb(work, "u2", [P, UT, S])
        q2 = sb(work, "q2", [P, UT, S])
        keys_ = ExitStack()
        kz = sb(keys_, "kz", [P, HEADS2, S])
        keys_.close()
        wg = sb(work, "wg", [P, UT, 512])
        v2 = sb(work, "v2", [P, TT, 512])
        bbT = sb(work, "bbT", [P, 2, UT, P])
        vin = sb(work, "vin", [P, 2, S])
        ysc = sb(work, "ysc", [P, 3, 2, S])
        mc = sb(work, "mc", [P, 2, 2, S])
        ms = sb(work, "ms", [P, 2, 2, S])
        y2 = sb(work, "y2", [P, UT, S])
        sq2 = q2
        pm2 = gate_b[:, 0:768].rearrange("p (h n) -> p h n", h=2)
        pT2 = row_b[:, 0:768].rearrange("p (h n) -> p h n", h=2)
        sig = hT[:, 0:UT, :]
        rmax2 = sb(work, "rmax2", [P, HEADS2, 2])
        negm2 = sb(work, "negm2", [P, HEADS2, 2])
        psum2 = sb(work, "psums2", [P, 2, HEADS2])
        prec2 = sb(work, "prec2", [P, 2, HEADS2])
        work.close()
        pos_i = xn[:, 1, 0:S].bitcast(I32)
        work = ExitStack()
        sb(work, "behind", [P, 10 * 1024])
        rot4 = sb(work, "rot4", [P, 2, 2, P])
        wpow = sb(work, "wpow", [P, 6, ST])
        work.close()

        gu_bank = [bank("gu_bank0"), bank("gu_bank1")]
        yb = [bank(f"y_bank{n}") for n in range(4)]
        tb = [bank("t_bank0"), bank("t_bank1")]
        zb = [*gu_bank, *tb]

        x_loaded, cst_loaded, masks_loaded, pos_loaded, lc_loaded = sem("x_loaded"), sem("cst_loaded"), sem("masks_loaded"), sem("pos_loaded"), sem("lc_loaded")
        pro_loaded = [sem(f"pro_loaded{n}") for n in range(8)]
        ada_loaded = [sem("ada_loaded0"), sem("ada_loaded1")]
        gu_loaded = [sem("gu_loaded0"), sem("gu_loaded1")]
        dn_loaded = [sem("dn_loaded0"), sem("dn_loaded1")]
        unit_loaded = [sem(f"unit_loaded{n}") for n in range(RING)]
        gbias_loaded, wg_loaded, row_loaded, final_loaded, stored = sem("gbias_loaded"), sem("wg_loaded"), sem("row_loaded"), sem("final_loaded"), sem("stored")
        dve_step, act_step, pool_step = sem("dve_step"), sem("act_step"), sem("pool_step")
        ones_set, c_ready, pro_done, pro_rows = sem("ones_set"), sem("c_ready"), sem("pro_done"), sem("pro_rows")
        prep_act, prep_args, prep_dve = sem("prep_act"), sem("prep_args"), sem("prep_dve")
        ada_step, piece_done = sem("ada_step"), sem("piece_done")
        mod_ps, mod_done, gate_ps, gate_done = sem("mod_ps"), sem("mod_done"), sem("gate_ps"), sem("gate_done")
        x_ready, rms_ready, xn_ready, tr_ready, hT_ready = sem("x_ready"), sem("rms_ready"), sem("xn_ready"), sem("tr_ready"), sem("hT_ready")
        hT_hi_done, hT_lo_done = sem("hT_hi_done"), sem("hT_lo_done")
        gu_hi_done, gu_lo_done, dn_hi_done, dn_lo_done = sem("gu_hi_done"), sem("gu_lo_done"), sem("dn_hi_done"), sem("dn_lo_done")
        gu_ps, silu_done, prod_done, act_hi_done, act_done, dn_used, y_ps = (
            sem("gu_ps"), sem("silu_done"), sem("prod_done"), sem("act_hi_done"), sem("act_done"), sem("dn_used"), sem("y_ps"))
        tile_ps, tile_out, wout_done, mix_done = sem("tile_ps"), sem("tile_out"), sem("wout_done"), sem("mix_done")
        w_hi_done, w_lo_done = sem("w_hi_done"), sem("w_lo_done")
        sq_ready, lat_ss, lat_rooted, lat_done = sem("sq_ready"), sem("lat_ss"), sem("lat_rooted"), sem("lat_done")
        kr_ready, qr_ready, diff_ready = sem("kr_ready"), sem("qr_ready"), sem("diff_ready")
        sc_ps, sm_done, negm_ready, p_ready, pn_ready = sem("sc_ps"), sem("sm_done"), sem("negm_ready"), sem("p_ready"), sem("pn_ready")
        tables_done, bb_ps, bb_done, bu_ps, bu_used, scanned, turned, states_done, c_ps, skip_done, v_used = (
            sem("tables_done"), sem("bb_ps"), sem("bb_done"), sem("bu_ps"), sem("bu_used"), sem("scanned"), sem("turned"), sem("states_done"),
            sem("c_ps"), sem("skip_done"), sem("v_used"))
        gelu_done, glu_ps, sig_done, glu_done, sq2_done, ssm_ss, ssm_rooted, mix2_done = (
            sem("gelu_done"), sem("glu_ps"), sem("sig_done"), sem("glu_done"), sem("sq2_done"), sem("ssm_ss"), sem("ssm_rooted"), sem("mix2_done"))
        sc2_ps, sm2_done, negm2_done, p2_done, pt_ps, pt_out, o_ps, o_done, o_rooted, on_done, ot_ps, kz_zero = (
            sem("sc2_ps"), sem("sm2_done"), sem("negm2_done"), sem("p2_done"), sem("pt_ps"), sem("pt_out"), sem("o_ps"), sem("o_done"),
            sem("o_rooted"), sem("on_done"), sem("ot_ps"), sem("kz_zero"))
        post_sq, post_rooted = sem("post_sq"), sem("post_rooted")

        block = ctx.enter_context(nc.Block())

        def half(b):
            return slice(512 * b, 512 * (b + 1))

        def tok(t):
            return slice(P * t, P * (t + 1))

        DVE_CHUNKS = (1, 4)
        PRO = 8 + len(DVE_CHUNKS)

        def pro_sums(n):
            return part[:, n // 4, S * (n % 4):S * (n % 4 + 1)]

        def pro_row(n):
            return [*yb, *gu_bank][n - sum(m < n for m in DVE_CHUNKS)][0:1, 0:S]

        def pro_slot(n):
            if n < 5:
                return pro[:, n, :, :]
            return ring[:, 0:2, :].rearrange("p a (b n) -> p (a b) n", n=S) if n == 5 else ada_in[:, n - 6, :, :]

        def unit_loaded_at(mixer, n):
            slot = n % RING
            return unit_loaded[slot], 16 * (-(-(UNITS - slot) // RING) * mixer + n // RING + 1)

        def split_used(l, m):
            if m < SPLITS - KC:
                q = ZT + 8
                return tile_ps, TILES * l + [*range(1, ZT + 1), ZT + 3, ZT + 6, q, q + HEADS, q + HEADS + POOLG + TT][m]
            return wout_done, (KC - 1) * l + m - (SPLITS - KC) + 1

        def split_used2(m):
            if m < 12:
                return tile_ps, TILES * DEPTH + m + 1
            if m < 15:
                return v_used, m - 11
            if m == 15:
                return tile_ps, TILES * DEPTH + 14
            return wout_done, (KC - 1) * DEPTH + m - 15

        NORMS = 3 * DEPTH

        @block.sync
        def _(sp_):
            def load_gu(g, b):
                sp_.dma_start(raw_gu[:, b, :], ffn_gu[bass.ds(g, 1)].rearrange("a p n -> p (a n)")).then_inc(gu_loaded[b], 16)

            def load_dn(g, b):
                sp_.dma_start(raw_dn[:, b, :], ffn_dn[bass.ds(g, 1)].rearrange("a p n -> p (a n)")).then_inc(dn_loaded[b], 16)

            def gate_bias(k, row):
                sp_.wait_ge(x_ready, 4 * k + 4)
                sp_.dma_start(gate_b[:, :], gate_rows[bass.ds(row, 1)].to_broadcast([P, D])).then_inc(gbias_loaded, 16)

            def next_block(base, n, b):
                sp_.wait_ge(gu_lo_done, base + n + 1)
                load_gu(base + n + 2, b)
                sp_.wait_ge(dn_lo_done, base + n + 1)
                load_dn(base + n + 2, b)

            def ffn_loads(base):
                with sp_.Fori(0, FB // 2 - 1) as i:
                    for b in range(2):
                        next_block(base, 2 * i + b, b)

            def first_blocks(base):
                for b in range(2):
                    next_block(base, FB - 2 + b, b)

            def units(src, at, which, used):
                for n in which:
                    if n >= RING:
                        sp_.wait_ge(*used(n - RING))
                    sp_.dma_start(ring[:, n % RING, :], src[bass.ds(at + n, 1)].rearrange("a p n -> p (a n)"))\
                       .then_inc(unit_loaded[n % RING], 16)

            def mixer_used(l):
                def used(n):
                    if n == POOL_UNIT:
                        return tile_ps, TILES * l + ZT + 8 + HEADS + POOLG
                    return w_lo_done, SPLITS * l + n - (n > POOL_UNIT) + 1
                return used

            def mixer2_used(n):
                return w_lo_done, SPLITS * DEPTH + n + 1

            sp_.dma_start(cst[:, 0:C_RATIO], consts[:, 0:C_RATIO]).then_inc(cst_loaded, 16)
            sp_.dma_start(pos_i, positions.to_broadcast([P, S])).then_inc(pos_loaded, 16)
            sp_.dma_start(lc[:, :], cols[0]).then_inc(lc_loaded, 16)
            for n in range(8):
                sp_.dma_start(pro_slot(n), ada[n].rearrange("p (c n) -> p c n", c=KC)).then_inc(pro_loaded[n], 16)
            sp_.dma_start(x[:, :, :], x_in.rearrange("(t p) d -> p t d", p=P)).then_inc(x_loaded, 16)
            for g in range(2):
                load_gu(g, g)
                load_dn(g, g)
            sp_.dma_start(cst[:, C_RATIO:C_N], consts[:, C_RATIO:C_N]).then_inc(masks_loaded, 16)
            with sp_.Fori(0, DEPTH) as l:
                gate_bias(3 * l, 3 * l)
                ffn_loads(2 * FB * l)
                units(mix_w, UNITS * l, range(RING), mixer_used(l))
                first_blocks(2 * FB * l)
                gate_bias(3 * l + 1, 3 * l + 1)
                units(mix_w, UNITS * l, range(RING, UNITS), mixer_used(l))
                gate_bias(3 * l + 2, 3 * l + 2)
                sp_.wait_ge(mod_done, 3 * l + 3)
                sp_.dma_start(lc[:, :], cols[bass.ds(l + 1, 1)].rearrange("a p n -> p (a n)")).then_inc(lc_loaded, 16)
                ffn_loads(2 * FB * l + FB)
                first_blocks(2 * FB * l + FB)
            sp_.wait_ge(gate_ps, 6 * DEPTH - 2)
            sp_.dma_start(row_b[:, :], rows[0:1].to_broadcast([P, D])).then_inc(final_loaded, 16)
            units(mix2_w, 0, range(19), mixer2_used)
            sp_.wait_ge(sc2_ps, HEADS2)
            for n in range(2):
                sp_.dma_start(wg[:, 2 * n:2 * n + 2, :], mix2_w[UNITS2 + n].rearrange("p (c n) -> p c n", c=2)).then_inc(wg_loaded, 16)
            units(mix2_w, 0, range(19, UNITS2), mixer2_used)
            sp_.wait_ge(o_ps, HEADS2)
            sp_.dma_start(row_b[:, :], rows[1:2].to_broadcast([P, D])).then_inc(row_loaded, 16)
            sp_.dma_start(gate_b[:, :], rows[2:3].to_broadcast([P, D])).then_inc(gbias_loaded, 16)
            ffn_loads(4 * FB)
            for t in range(TT):
                sp_.wait_ge(x_ready, 4 * NORMS + 14 + 2 * t)
                sp_.dma_start(out.rearrange("(t p) d -> p t d", p=P)[:, t, :], x[:, t, :]).then_inc(stored, 16)
            sp_.wait_ge(stored, 32)

        @block.gpsimd
        def _(pool):
            step = Steps(pool, pool_step)
            pool.memset(ones[:, :], 1.0).then_inc(ones_set, 1)
            pool.memset(tiny[:, 0:1], EPS).then_inc(ones_set, 1)
            pool.memset(part[:, 0:2, :], 0.0).then_inc(ones_set, 1)

            def fetch(q, b):
                pool.dma_start(ada_in[:, b, :, :], ada[bass.ds(q + 8, 1)].rearrange("a p (c n) -> p (a c) n", c=KC))\
                    .then_inc(ada_loaded[b], 16)

            def weigh(chunk, add_up, into):
                add_up(pool.tensor_tensor(chunk, chunk, c_act[:, :].unsqueeze(2).to_broadcast([P, KC, S]), ALU.mult))
                add_up(pool.tensor_tensor(chunk[:, 0:4, :], chunk[:, 0:4, :], chunk[:, 4:8, :], ALU.add))
                add_up(pool.tensor_tensor(chunk[:, 0:2, :], chunk[:, 0:2, :], chunk[:, 2:4, :], ALU.add))
                return pool.tensor_tensor(into, chunk[:, 0, :], chunk[:, 1, :], ALU.add)

            pool.sem_inc(piece_done, 1)
            pool.wait_ge(c_ready, 1)
            pool.wait_ge(pro_done, PRO)
            for b in range(2):
                fetch(b, b)

            order = []
            for l in range(DEPTH):
                order += [(4, gate_ps, 6 * l - 4), (2, mod_ps, 3 * l - 1), (3, mod_ps, 3 * l - 1), (5, gate_ps, 6 * l - 2),
                          (0, mod_ps, 3 * l + 1), (1, mod_ps, 3 * l + 1), (6, gate_ps, 6 * l)]
                if l < DEPTH - 1:
                    order += [(0, mod_ps, 3 * l + 3), (1, mod_ps, 3 * l + 3)]
            for n, (slot, used, count) in enumerate(order):
                if count > 0:
                    pool.wait_ge(used, count)

                def chunk(i, b, more):
                    q = 4 * n + 2 * i + b
                    done = [0]

                    def own(instruction):
                        instruction.then_inc(ada_step, 1)
                        done[0] += 1
                        pool.wait_ge(ada_step, 4 * q + done[0])

                    pool.wait_ge(ada_loaded[b], 32 * n + 16 * i + 16)
                    own(weigh(ada_in[:, b, :, :], own, part[:, slot, bass.ds(2 * S * i + S * b, S)]))
                    if more:
                        fetch(q + 2, b)

                if n < len(order) - 1:
                    with pool.Fori(0, 2) as i:
                        for b in range(2):
                            chunk(i, b, True)
                else:
                    for i in range(2):
                        for b in range(2):
                            chunk(i, b, i == 0)
                pool.sem_inc(piece_done, 1)

            pool.wait_ge(mod_ps, 3 * DEPTH)
            pool.wait_ge(gate_ps, 6 * DEPTH - 2)
            pool.wait_ge(prep_dve, 1)
            pool.wait_ge(masks_loaded, 16)
            step.did(pool.memset(bbd[:, :, :, :, :, :], 0.0))
            step.then(pool.memset(cz[:, :, :, :, :], 0.0))
            bre, bim = (cst[:, c:c + 256].rearrange("p (s h) -> p s h", h=16) for c in (C_BRE, C_BIM))
            c_re, c_im = (cst[:, c:c + 256].rearrange("p (s h) -> p s h", h=16) for c in (C_CRE, C_CIM))
            t1 = ecos[:, 0, :].rearrange("p (s h) -> p s h", h=16)
            t2 = ecos[:, 1, :].rearrange("p (s h) -> p s h", h=16)
            wide = [P, ST, 16]
            for r, (fr, fi, op) in enumerate(((bre, bim, ALU.subtract), (bim, bre, ALU.add))):
                step.did(pool.tensor_tensor(t1, fr, cre[:, :].unsqueeze(2).to_broadcast(wide), ALU.mult))
                step.then(pool.tensor_tensor(t2, fi, cim[:, :].unsqueeze(2).to_broadcast(wide), ALU.mult))
                for g in range(2):
                    rows_ = slice(64 * g, 64 * g + 64)
                    to = bbd[rows_, r, :, :, g, :].rearrange("p u j h -> p (u j) h")
                    step.then(pool.tensor_tensor(to, t1[rows_], t2[rows_], op))
            for n, (src, sign) in enumerate(((c_re, 1.0), (c_im, -1.0))):
                for g in range(2):
                    rows_ = slice(64 * g, 64 * g + 64)
                    step.then(pool.tensor_scalar(cz[rows_, n, :, g, :], src[rows_], sign, None, ALU.mult))
            step.did(pool.memset(ecos[:, :, 0:1], 1.0))
            step.did(pool.memset(esin[:, :, 0:1], 0.0))
            step.did(pool.tensor_copy(wpow[:, 0, :], cos1[:, :]))
            step.then(pool.tensor_copy(wpow[:, 1, :], sin1[:, :]))
            n = 1
            while n < S:
                for s in range(0, ST, 2):
                    e_c, e_s = ecos[:, s:s + 2, 0:n], esin[:, s:s + 2, 0:n]
                    w_c, w_s = (wpow[:, a, s:s + 2].unsqueeze(2).to_broadcast([P, 2, n]) for a in (0, 1))
                    o1, o2 = rot4[:, 0, :, 0:n], rot4[:, 1, :, 0:n]
                    step.did(pool.tensor_tensor(o1, e_c, w_c, ALU.mult))
                    step.then(pool.tensor_tensor(o2, e_s, w_s, ALU.mult))
                    step.then(pool.tensor_tensor(ecos[:, s:s + 2, n:2 * n], o1, o2, ALU.subtract))
                    step.did(pool.tensor_tensor(o1, e_c, w_s, ALU.mult))
                    step.then(pool.tensor_tensor(o2, e_s, w_c, ALU.mult))
                    step.then(pool.tensor_tensor(esin[:, s:s + 2, n:2 * n], o1, o2, ALU.add))
                step.did(pool.tensor_tensor(wpow[:, 2, :], wpow[:, 0, :], wpow[:, 0, :], ALU.mult))
                step.did(pool.tensor_tensor(wpow[:, 3, :], wpow[:, 1, :], wpow[:, 1, :], ALU.mult))
                step.then(pool.tensor_tensor(wpow[:, 4, :], wpow[:, 0, :], wpow[:, 1, :], ALU.mult))
                step.did(pool.tensor_tensor(wpow[:, 0, :], wpow[:, 2, :], wpow[:, 3, :], ALU.subtract))
                step.then(pool.tensor_tensor(wpow[:, 1, :], wpow[:, 4, :], wpow[:, 4, :], ALU.add))
                n *= 2
            pool.sem_inc(tables_done, 1)

            pool.wait_ge(x_ready, 4 * NORMS + 4)
            for h in range(HEADS2):
                pool.memset(kz[64 * (1 - h % 2):64 * (2 - h % 2), h, :], 0.0).then_inc(kz_zero, 1)
                pool.wait_ge(kz_zero, h + 1)
            for s in range(ST):
                pool.wait_ge(scanned, s + 1)
                if s >= 2:
                    pool.wait_ge(c_ps, s - 1)
                for to, table in ((mc, ecos), (ms, esin)):
                    pool.tensor_tensor(to[:, s % 2, :, :], ysc[:, s % 3, :, :],
                                       table[:, s, :].unsqueeze(1).to_broadcast([P, 2, S]), ALU.mult).then_inc(turned, 1)
                pool.wait_ge(turned, 2 * s + 2)
                pool.tensor_tensor(mc[:, s % 2, 0, :], mc[:, s % 2, 0, :], ms[:, s % 2, 1, :], ALU.subtract).then_inc(states_done, 1)
                pool.tensor_tensor(mc[:, s % 2, 1, :], mc[:, s % 2, 1, :], ms[:, s % 2, 0, :], ALU.add).then_inc(states_done, 1)

        @block.tensor
        def _(pe):
            def modulation(k, l, m):
                pe.wait_ge(piece_done, 9 * l + 3 * m + 1)
                pe.wait_ge(gate_done, 2 * k + 2)
                for j in range(16):
                    if m == 0 and j % KC == 0:
                        pe.wait_ge(pro_done, PRO // 2 * (j // KC + 1))
                    last = pe.matmul(tb[0][:, j:j + 1], part[:, 2 * (m == 1) + j // KC, tok(j % KC)], ones[:, 0:1], start=True, stop=True)
                last.then_inc(mod_ps, 1)

            def transposes(k):
                for t in range(TT):
                    pe.wait_ge(xn_ready, 2 * k + t + 1)
                    for c in range(KC):
                        last = pe.transpose(yb[c // 2][:, S * (c % 2) + P * t:S * (c % 2) + P * (t + 1)], xn[:, t, tok(c)], ident)
                        if t == TT - 1 and c % 2:
                            last.then_inc(tr_ready, 1)

            def passes(to, a, b, start, stop):
                pe.matmul(to, a[0], b[0], start=start, stop=False)
                pe.matmul(to, a[0], b[1], start=False, stop=False)
                return pe.matmul(to, a[1], b[0], start=False, stop=stop)

            def split_unit(mixer, m):
                pe.wait_ge(w_lo_done, SPLITS * mixer + m + 1)
                return dn_hi[:, (m + 2) % SLOTS, :], dn_lo[:, (m + 2) % SLOTS, :]

            def product(to, w, kt=None):
                for c in range(KC):
                    if kt is not None and c % 2 == 0:
                        pe.wait_ge(hT_lo_done, 4 * kt + c // 2 + 1)
                    last = passes(to, [a[:, tok(c)] for a in w], (hT_hi[:, c, :], hT_lo[:, c, :]), c == 0, c == KC - 1)
                return last

            def gate(l, m):
                pe.wait_ge(piece_done, 9 * l + 3 * m + 2)
                for b in range(2):
                    pe.matmul(tb[b][:, :], ones[:, :], part[:, 4 + m, half(b)], start=True, stop=True).then_inc(gate_ps, 1)

            def ffn(f, kt, in_between=None):
                base = FB * f

                def gate_up(n, b, n_first=None):
                    pe.wait_ge(gu_lo_done, base + n + 1)
                    if n_first is None:
                        pe.wait_ge(prod_done, base + n - 1)
                    for h in range(2):
                        for c in range(KC):
                            if n_first == 0 and h == 0 and c % 2 == 0:
                                pe.wait_ge(hT_lo_done, 4 * kt + c // 2 + 1)
                            last = passes(gu_bank[b][:, S * h:S * (h + 1)], (gu_hi[:, b, h, c, :], gu_lo[:, b, h, c, :]),
                                          (hT_hi[:, c, :], hT_lo[:, c, :]), c == 0, c == KC - 1)
                    last.then_inc(gu_ps, 1)

                def down(n, b, first=False, final=False):
                    pe.wait_ge(dn_lo_done, base + n + 1)
                    pe.wait_ge(act_done, base + n + 1)
                    for t in range(TT):
                        for h in range(2):
                            last = passes(yb[2 * t + h][:, :], (act_hi[:, b, tok(t)], act_lo[:, b, tok(t)]),
                                          (dn_hi[:, b, half(h)], dn_lo[:, b, half(h)]), first, final)
                            if final:
                                last.then_inc(y_ps, 1)
                    if not final:
                        last.then_inc(dn_used, 1)

                gate_up(0, 0, 0)
                gate_up(1, 1, 1)
                down(0, 0, first=True)
                for part_, blocks in enumerate(((0, FB // 4), (FB // 4, FB // 2 - 1))):
                    if part_ and in_between:
                        in_between()
                    with pe.Fori(*blocks) as i:
                        for b in range(2):
                            gate_up(2 * i + b + 2, b)
                            down(2 * i + b + 1, 1 - b)
                down(FB - 1, 1, final=True)

            def mixer(l):
                base = TILES * l
                seen = [0]

                def tile_bank():
                    n = seen[0]
                    seen[0] += 1
                    if n >= 4:
                        pe.wait_ge(tile_out, base + n - 3)
                    return zb[n % 4]

                def z_tile(n):
                    product(tile_bank()[:, 0:S], split_unit(l, n), 3 * l + 1 if n == 0 else None).then_inc(tile_ps, 1)

                def mean_square(a, chunks):
                    pe.wait_ge(sq_ready, (QCH + KVCH) * l + chunks.stop)
                    for c in chunks:
                        last = pe.matmul(yb[a][:, 0:S], ones[:, :], sq[:, c, :], start=c == chunks.start, stop=c == chunks.stop - 1)
                    last.then_inc(lat_ss, 1)

                for n in range(ZT):
                    z_tile(n)
                    if n == 3:
                        mean_square(0, range(QCH))
                    elif n == 5:
                        mean_square(1, range(QCH, QCH + KVCH))

                def latent(c, cols_=slice(0, S)):
                    return lat_hi[:, c, cols_], lat_lo[:, c, cols_]

                pe.wait_ge(lat_done, 2 * l + 1)
                for n in range(8):
                    to = tile_bank()
                    for c in range(QCH):
                        m, piece = divmod(QCH * n + c, KC)
                        if piece == 0:
                            w = split_unit(l, ZT + m)
                        last = passes(to[:, 0:S], [a[:, tok(piece)] for a in w], latent(c), c == 0, c == QCH - 1)
                    last.then_inc(tile_ps, 1)
                w = split_unit(l, ZT + QCH)
                pe.wait_ge(lat_done, 2 * l + 2)
                for n in range(HEADS):
                    to = tile_bank()
                    for c in range(KVCH):
                        last = passes(to[:, 0:S], [a[:, tok(KVCH * n + c)] for a in w], latent(QCH + c), c == 0, c == KVCH - 1)
                    last.then_inc(tile_ps, 1)
                pe.wait_ge(*unit_loaded_at(l, POOL_UNIT))
                pe.wait_ge(diff_ready, POOLG * l + POOLG)
                for g, sums in enumerate((sumA[:, 0], sumB[:, 0], sumA[:, 2], sumB[:, 2])):
                    to = tile_bank()
                    pe.matmul(to[:, 0:S], ring[:, POOL_UNIT % RING, tok(g)], sums[:, PADT:PADT + S], start=True, stop=True).then_inc(tile_ps, 1)
                w = split_unit(l, ZT + QCH + 1)
                for t in range(TT):
                    to = tile_bank()
                    for c in range(KVCH):
                        last = passes(to[:, :], latent(QCH + c, tok(t)), [a[:, half(c)] for a in w], c == 0, c == KVCH - 1)
                    last.then_inc(tile_ps, 1)

                pe.wait_ge(tile_out, base + ZT + 8 + HEADS)
                pe.wait_ge(kr_ready, 2 * l + 2)
                pe.wait_ge(qr_ready, l + 1)
                for h in range(HEADS):
                    pe.wait_ge(tile_out, base + seen[0] - 3 + h)
                    bank_ = zb[(seen[0] + h) % 4]
                    for t in range(TT):
                        to = bank_[:, 0:P] if t == 0 else bank_[:, P:P + S]
                        keys = slice(0, P * (t + 1))
                        pe.matmul(to, qn[:, h, tok(t)], kn[:, h, keys], start=True, stop=False)
                        last = pe.matmul(to, qr[:, h // 2, tok(t)], krz[:, h % 2, keys], start=False, stop=True)
                    last.then_inc(sc_ps, 1)
                def w_out(c):
                    w = split_unit(l, SPLITS - KC + c)
                    pe.wait_ge(mix_done, KC * l + c + 1)
                    for t in range(TT):
                        for b in range(2):
                            last = passes(yb[2 * t + b][:, :], (hT_hi[:, c, tok(t)], hT_lo[:, c, tok(t)]), [a[:, half(b)] for a in w],
                                          c == 0, c == KC - 1)
                            if c == KC - 1:
                                last.then_inc(y_ps, 1)
                    if c < KC - 1:
                        last.then_inc(wout_done, 1)

                pe.wait_ge(lat_rooted, 2 * l + 2)
                for c in range(POOLG):
                    w_out(c)

                def turn(h):
                    to = tile_bank()
                    pe.wait_ge(pn_ready, 2 * HEADS * l + 2 * h + 2)
                    for c in range(3):
                        last = pe.transpose(to[:, tok(c)], pm[:, h, tok(c)], ident)
                    last.then_inc(tile_ps, 1)

                def head_out(h, turned_at):
                    to = tile_bank()
                    pe.wait_ge(tile_out, base + turned_at + 1)
                    pe.matmul(to[:, 0:S], v[:, 0, tok(h)], pT[:, h, 0:S], start=True, stop=False)
                    pe.matmul(to[:, P:S], v[:, 1, tok(h)], pT[:, h, S:S + P], start=False, stop=True).then_inc(tile_ps, 1)

                pe.wait_ge(sm_done, HEADS * (l + 1))
                turned_at = {}
                for h in range(HEADS):
                    turned_at[h] = seen[0]
                    turn(h)
                    if h:
                        head_out(h - 1, turned_at[h - 1])
                head_out(HEADS - 1, turned_at[HEADS - 1])
                assert seen[0] == TILES

                for c in range(POOLG, KC):
                    if c == KC - 1:
                        gate(l, 1)
                    w_out(c)

            pe.wait_ge(c_ready, 1)
            for n in range(8):
                if n not in DVE_CHUNKS:
                    pe.wait_ge(pro_loaded[n], 16)
                    for c in range(KC):
                        last = pe.matmul(pro_row(n), c_act[:, c:c + 1], pro_slot(n)[:, c, :], start=c == 0, stop=c == KC - 1)
                    last.then_inc(pro_rows, 1)
            pe.wait_ge(ones_set, 3)
            pe.wait_ge(cst_loaded, 16)
            with pe.Fori(0, DEPTH) as l:
                for m in range(3):
                    modulation(3 * l + m, l, m)
                    transposes(3 * l + m)
                    if m == 1:
                        mixer(l)
                    else:
                        ffn(2 * l + m // 2, 3 * l + m, lambda: gate(l, m))

            base = TILES * DEPTH
            pe.wait_ge(tables_done, 1)
            pe.wait_ge(gate_done, 6 * DEPTH + 2)
            for r in range(2):
                for u in range(UT):
                    last = pe.transpose(tb[r][:, tok(u)], bbd[:, r, u, :, :, :].rearrange("p j g h -> p (j g h)"), ident)
                last.then_inc(bb_ps, 1)
            transposes(3 * DEPTH)

            def col_tile(n):
                if n >= 4:
                    pe.wait_ge(tile_out, base + n - 3)
                elif n >= 2:
                    pe.wait_ge(bb_done, 2)
                product(zb[n % 4][:, 0:S], split_unit(DEPTH, n), 3 * DEPTH if n == 0 else None).then_inc(tile_ps, 1)

            def value_unit(m):
                pe.wait_ge(tile_out, base + 10)
                w = split_unit(DEPTH, 12 + m)
                for c in (2 * m, 2 * m + 1):
                    for t in range(TT):
                        last = passes(zb[t][:, :], (hT_hi[:, c, tok(t)], hT_lo[:, c, tok(t)]), [a[:, half(c % 2)] for a in w], c == 0, c == KC - 1)
                        if c == KC - 1:
                            last.then_inc(tile_ps, 1)
                if m < 3:
                    last.then_inc(v_used, 1)

            def inputs(s):
                u, rows_ = s // 4, slice(32 * (s % 4), 32 * (s % 4) + 32)
                if s >= 2:
                    pe.wait_ge(bu_used, 2 * (s - 1))
                for r in range(2):
                    last = pe.matmul(yb[s % 2][:, S * r:S * (r + 1)], bbT[rows_, r, u, :], u2[rows_, u, :], start=True, stop=True)
                last.then_inc(bu_ps, 1)

            def outputs(s):
                u, rows_ = s // 4, slice(32 * (s % 4), 32 * (s % 4) + 32)
                to = yb[2 + u % 2][rows_, 0:S]
                if s % 4 == 0 and u >= 2:
                    pe.wait_ge(skip_done, u - 1)
                for r in range(2):
                    pe.wait_ge(states_done, 2 * s + r + 1)
                    last = pe.matmul(to, cz[:, r, s, :, :].rearrange("p g h -> p (g h)"), mc[:, s % 2, r, :], start=r == 0, stop=r == 1)
                last.then_inc(c_ps, 1)

            tri = mask[:, 0:P]

            def scores(h):
                if h == 0:
                    pe.wait_ge(tile_out, base + 12)
                    pe.wait_ge(kz_zero, HEADS2)
                elif h >= 2:
                    pe.wait_ge(pt_out, h - 1)
                to = zb[2 + h % 2]
                pe.matmul(to[:, 0:P], q2[:, h // 2, tok(0)], kz[:, h, 0:P], start=True, stop=False)
                pe.matmul(to[:, 0:P], ident, tri, start=False, stop=True)
                pe.matmul(to[:, P:P + S], q2[:, h // 2, tok(1)], kz[:, h, :], start=True, stop=False)
                pe.matmul(to[:, S:S + P], ident, tri, start=False, stop=True).then_inc(sc2_ps, 1)

            def turn2(h):
                pe.wait_ge(p2_done, 2 * h + 2)
                for c in range(3):
                    last = pe.transpose(zb[2 + h % 2][:, tok(c)], pm2[:, h % 2, tok(c)], ident)
                last.then_inc(pt_ps, 1)

            def head_out2(h):
                pe.wait_ge(pt_out, h + 1)
                pe.wait_ge(tile_out, base + 14)
                cols_ = slice(HD2 * h, HD2 * (h + 1))
                pe.matmul(zb[0][:, cols_], pT2[:, h % 2, 0:P], v2[:, 0, cols_], start=True, stop=True)
                pe.matmul(zb[1][:, cols_], pT2[:, h % 2, P:S], v2[:, 0, cols_], start=True, stop=False)
                pe.matmul(zb[1][:, cols_], pT2[:, h % 2, S:S + P], v2[:, 1, cols_], start=False, stop=True).then_inc(o_ps, 1)

            for n in range(4):
                col_tile(n)
            pe.wait_ge(tile_out, base + 4)
            inputs(0)
            inputs(1)
            for s in range(ST):
                if s < 8:
                    col_tile(4 + s)
                elif s < 12:
                    value_unit(s - 8)
                if s >= 1:
                    outputs(s - 1)
                if s + 2 < ST:
                    inputs(s + 2)
                for stage, first in ((head_out2, 11), (turn2, 10), (scores, 8)):
                    if s >= first and (s - first) % 2 == 0:
                        stage(s - first)
                        stage(s - first + 1)
            outputs(ST - 1)
            for stage in (turn2, head_out2):
                stage(HEADS2 - 2)
                stage(HEADS2 - 1)

            pe.wait_ge(wg_loaded, 32)
            pe.wait_ge(bu_used, 2 * ST)

            def glu(e, c):
                pe.wait_ge(gelu_done, c + 1)
                last = pe.matmul(yb[e][:, 0:S], wg[:, c, tok(e)], y2[:, c, :], start=c == 0, stop=c == UT - 1)
                if c == UT - 1:
                    last.then_inc(glu_ps, 1)

            def w_out(i):
                c = (UT + i) % KC
                w = split_unit(DEPTH, 16 + i)
                pe.wait_ge(mix2_done, max(2, i // 2 + 1))
                for t in range(TT):
                    for b in range(2):
                        last = passes(zb[2 * t + b][:, :], (hT_hi[:, c, tok(t)], hT_lo[:, c, tok(t)]), [a[:, half(b)] for a in w], i == 0, i == KC - 1)
                        if i == KC - 1:
                            last.then_inc(y_ps, 1)
                if i < KC - 1:
                    last.then_inc(wout_done, 1)

            for c in range(2):
                for e in range(2):
                    glu(e, c)
            for t in range(TT):
                pe.wait_ge(on_done, t + 1)
                for c in range(4):
                    last = pe.transpose(tb[c // 2][:, S * (c % 2) + P * t:S * (c % 2) + P * (t + 1)], xn[:, t, 512 + P * c:512 + P * (c + 1)], ident)
                    if t == TT - 1 and c % 2:
                        last.then_inc(ot_ps, 1)
            for c in (2, 3):
                for e in range(2):
                    glu(e, c)
            for e in (2, 3):
                for c in range(UT):
                    glu(e, c)
            w_out(0)
            w_out(1)
            pe.wait_ge(sq2_done, UT)
            for c in range(UT):
                last = pe.matmul(yb[2][:, 0:S], ones[:, :], sq2[:, c, :], start=c == 0, stop=c == UT - 1)
            last.then_inc(ssm_ss, 1)
            for i in range(2, KC):
                w_out(i)

            transposes(3 * DEPTH + 1)
            ffn(NFFN - 1, 3 * DEPTH + 1)

        @block.scalar
        def _(act):
            step = Steps(act, act_step)
            eps = tiny[:, 0:1]

            def table(func):
                step.then(act.activation(junk[:, :], eps, func))

            def norm(k):
                for t in range(TT):
                    a, b = ss[:, 2 * t:2 * t + 1], ss[:, 2 * t + 1:2 * t + 2]
                    act.wait_ge(x_ready, 4 * k + 2 * t + 1)
                    step.then(act.activation(xn[:, t, half(0)], x[:, t, half(0)], ACT.Square, accum_out=a))
                    step.did(act.activation(a, a, ACT.Identity, bias=eps, scale=1.0 / D))
                    act.wait_ge(x_ready, 4 * k + 2 * t + 2)
                    step.then(act.activation(xn[:, t, half(1)], x[:, t, half(1)], ACT.Square, accum_out=b))
                    act.activation(rms[:, t:t + 1], b, ACT.Sqrt, bias=a, scale=1.0 / D).then_inc(rms_ready, 1)

            def modulated(kt, gain, shift=None):
                def hi(j):
                    pair = slice(2 * j, 2 * j + 2)
                    act.activation(hT_hi[:, pair, :], hT[:, pair, :], ACT.Copy).then_inc(hT_hi_done, 1)

                for j in (0, 2):
                    act.wait_ge(tr_ready, 4 * kt + j + 1)
                    for c in (2 * j, 2 * j + 1):
                        src = yb[j][:, S * (c % 2):S * (c % 2 + 1)]
                        if shift is None:
                            step.did(act.activation(hT[:, c, :], src, ACT.Copy, scale=gain[:, c:c + 1]))
                        else:
                            step.did(act.activation(hT[:, c, :], src, ACT.Identity, scale=gain[:, c:c + 1], bias=shift[:, c:c + 1]))
                    step.settle()
                    hi(j)
                    act.wait_ge(hT_ready, 4 * kt + j + 2)
                    hi(j + 1)

            def split_unit(mixer, m, n, used):
                act.wait_ge(*unit_loaded_at(mixer, n))
                if used:
                    act.wait_ge(*used)
                act.activation(dn_hi[:, (m + 2) % SLOTS, :], ring[:, n % RING, :], ACT.Copy).then_inc(w_hi_done, 1)

            def split(l, m):
                split_unit(l, m, m + (m >= POOL_UNIT), split_used(l, m - SLOTS) if m >= SLOTS else None)

            def split2(m):
                split_unit(DEPTH, m, m, split_used2(m - SLOTS) if m >= SLOTS else None)

            def ffn(f, modulate, split_first):
                base = FB * f

                def split_gu(n, b, half_n, reused):
                    act.wait_ge(gu_loaded[b], 8 * base + 16 * half_n + 16)
                    if reused:
                        act.wait_ge(gu_ps, base + n - 1)
                    act.activation(gu_hi[:, b, :, :, :].rearrange("p h c n -> p (h c n)"), raw_gu[:, b, :], ACT.Copy).then_inc(gu_hi_done, 1)

                def split_dn(n, b, half_n, reused):
                    act.wait_ge(dn_loaded[b], 8 * base + 16 * half_n + 16)
                    if reused:
                        act.wait_ge(dn_used, (FB - 1) * f + n - 1)
                    act.activation(dn_hi[:, b, :], raw_dn[:, b, :], ACT.Copy).then_inc(dn_hi_done, 1)

                def silu(n, b, reused=True):
                    act.wait_ge(gu_ps, base + n + 1)
                    if reused:
                        act.wait_ge(prod_done, base + n - 1)
                    act.activation(sg[:, b, :], gu_bank[b][:, 0:S], ACT.Silu).then_inc(silu_done, 1)

                if split_first:
                    split_gu(0, 0, 0, False)
                modulate()
                split_dn(0, 0, 0, False)
                split_gu(1, 1, 0, False)
                for b in range(2):
                    silu(b, b, reused=False)
                    split_gu(b + 2, b, 1, True)
                    split_dn(b + 1, 1 - b, b, b == 1)
                with act.Fori(1, FB // 2 - 1) as i:
                    for b in range(2):
                        silu(2 * i + b, b)
                        split_gu(2 * i + b + 2, b, i + 1, True)
                        split_dn(2 * i + b + 1, 1 - b, i + b, True)
                silu(FB - 2, 0)
                split_dn(FB - 1, 1, FB // 2 - 1, True)
                silu(FB - 1, 1)

            def mixer(l):
                base = TILES * l
                seen = [0]

                def take(func, to, width=S, **more):
                    n = seen[0]
                    seen[0] += 1
                    act.wait_ge(tile_ps, base + n + 1)
                    act.activation(to, zb[n % 4][:, 0:width], func, **more).then_inc(tile_out, 1)

                def softmax(h):
                    act.wait_ge(negm_ready, HEADS * l + h + 1)
                    for t, part_ in enumerate((slice(0, P), slice(P, P + S))):
                        act.activation(pm[:, h, part_], pm[:, h, part_], ACT.Exp, bias=negm[:, h, t:t + 1], scale=MLA_SCALE,
                                       accum_out=psum_[:, h, t:t + 1]).then_inc(p_ready, 1)

                def mixed(c, **more):
                    act.wait_ge(tile_ps, base + seen[0] + 1)
                    act.activation(hT_hi[:, c, :], zb[seen[0] % 4][:, 0:S], ACT.Copy, **more)
                    take(ACT.Copy, hT[:, c, :], **more)

                for n in range(ZT):
                    split(l, n + SLOTS)
                    if n < QCH + KVCH:
                        act.activation(sq[:, n, :], zb[n % 4][:, 0:S], ACT.Square).then_inc(sq_ready, 1)
                    if n < 5:
                        take(ACT.Copy, z[:, n, :])
                    elif n < 9:
                        take(ACT.Copy, upad[:, n - 5, PADT:PADT + S])
                    else:
                        take(ACT.Copy, z[:, n - 4, :])
                    if n in (3, 5):
                        a, chunks = ((0, QCH), (1, KVCH))[n // 5]
                        act.wait_ge(lat_ss, 2 * l + a + 1)
                        act.activation(lat_rms[:, a, :], yb[a][:, 0:S], ACT.Sqrt, bias=eps, scale=1.0 / (P * chunks)).then_inc(lat_rooted, 1)
                for n in range(8):
                    take(ACT.Copy, qn[:, n, :] if n < HEADS else qrs[:, n - HEADS, :])
                    if n in (2, 5):
                        split(l, ZT + SLOTS + (2, 5).index(n))
                table(ACT.Exp)
                for h in range(HEADS):
                    take(ACT.Copy, kn[:, h, :])
                for g in range(POOLG):
                    mixed(g, scale=lc[:, L_PSC + g:L_PSC + g + 1])
                for t in range(TT):
                    take(ACT.Copy, v[:, t, :], 512)
                split(l, SPLITS - KC)
                softmax(0)
                split(l, SPLITS - KC + 1)
                softmax(1)
                split(l, SPLITS - KC + 2)
                softmax(2)
                softmax(3)
                for c in range(3):
                    split(l, SPLITS - KC + SLOTS + c)
                take(ACT.Copy, pT[:, 0, :], 384)
                split(l, SPLITS - KC + SLOTS + 3)
                for h in range(1, HEADS):
                    take(ACT.Copy, pT[:, h, :], 384)
                    mixed(POOLG + h - 1)
                mixed(POOLG + HEADS - 1)
                assert seen[0] == TILES
                table(ACT.Sqrt)
                split(l, SPLITS - 1)

            act.wait_ge(cst_loaded, 16)
            act.activation(c_act[:, :], cst[:, C_C:C_C + KC], ACT.Silu).then_inc(c_ready, 1)
            act.activation(sp[:, 0, :], cst[:, C_DT:C_DT + ST], ACT.Exp).then_inc(prep_act, 1)
            act.wait_ge(prep_args, 1)
            act.activation(mag[:, :], sp[:, 1, :], ACT.Exp).then_inc(prep_act, 1)
            for to, arg in ((sin1, sp[:, 3, :]), (cos1, sp[:, 4, :]), (sinT, xn[:, 0, 0:S]), (cosT, xn[:, 0, S:2 * S])):
                act.activation(to[:, :], arg, ACT.Sin).then_inc(prep_act, 1)
            act.wait_ge(ones_set, 3)
            table(ACT.Sqrt)

            with act.Fori(0, DEPTH) as l:
                step.enter_layers(l, ACT_LAYER)
                for m in range(3):
                    k = 3 * l + m

                    def modulate():
                        act.wait_ge(mod_done, k + 1)
                        modulated(k, gs, mods)

                    if m == 0:
                        norm(k)
                        act.wait_ge(pro_done, PRO)
                        ffn(2 * l, modulate, True)
                        split(l, 0)
                        table(ACT.Sqrt)
                        norm(k + 1)
                        split(l, 1)
                        split(l, 2)
                    elif m == 1:
                        modulate()
                        mixer(l)
                        act.wait_ge(gu_loaded[0], 8 * FB * (2 * l + 1) + 16)
                        act.activation(gu_hi[:, 0, :, :, :].rearrange("p h c n -> p (h c n)"), raw_gu[:, 0, :], ACT.Copy).then_inc(gu_hi_done, 1)
                        norm(k + 1)
                    else:
                        ffn(2 * l + 1, modulate, False)
                        table(ACT.Sqrt)
                step.leave_layers()

            split2(0)
            norm(NORMS)
            split2(1)
            split2(2)
            norm(NORMS + 1)
            for r in range(2):
                act.wait_ge(bb_ps, r + 1)
                act.activation(bbT[:, r, :, :], tb[r][:, :], ACT.Copy).then_inc(bb_done, 1)
            modulated(NORMS, lc[:, B_MIX:B_MIX + KC])
            base = TILES * DEPTH
            for n in range(12):
                split2(n + SLOTS)
                act.wait_ge(tile_ps, base + n + 1)
                src = zb[n % 4]
                if n < 8:
                    last = act.activation((u2 if n < 4 else q2)[:, n % 4, :], src[:, 0:S], ACT.Copy)
                else:
                    for h in (2 * (n - 8), 2 * (n - 8) + 1):
                        rows_ = slice(64 * (h % 2), 64 * (h % 2) + 64)
                        last = act.activation(kz[rows_, h, :], src[rows_, 0:S], ACT.Copy)
                        if h % 2 == 0:
                            step.did(last)
                last.then_inc(tile_out, 1)

            def gelu(u):
                act.wait_ge(skip_done, u + 1)
                act.activation(y2[:, u, :], y2[:, u, :], ACT.Gelu_apprx_tanh).then_inc(gelu_done, 1)

            def softmax(h):
                act.wait_ge(negm2_done, h + 1)
                for t, part_ in enumerate((slice(0, P), slice(P, P + S))):
                    act.activation(pm2[:, h % 2, part_], zb[2 + h % 2][:, part_], ACT.Exp, bias=negm2[:, h, t:t + 1], scale=HD2 ** -0.5,
                                   accum_out=psum2[:, t, h:h + 1]).then_inc(p2_done, 1)

            def turned_out(h):
                act.wait_ge(pt_ps, h + 1)
                if h >= 2:
                    act.wait_ge(o_ps, h - 1)
                act.activation(pT2[:, h % 2, :], zb[2 + h % 2][:, 0:384], ACT.Copy).then_inc(pt_out, 1)

            split2(15)
            gelu(0)
            gelu(1)
            table(ACT.Exp)
            for pair in range(HEADS2 // 2):
                softmax(2 * pair)
                softmax(2 * pair + 1)
                turned_out(2 * pair)
                turned_out(2 * pair + 1)
                if pair == 0:
                    split2(16)
                    for t in range(TT):
                        act.wait_ge(tile_ps, base + 13 + t)
                        act.activation(v2[:, t, :], zb[t][:, :], ACT.Copy).then_inc(tile_out, 1)
                    split2(17)
            split2(18)
            table(ACT.Sqrt)
            for t in range(TT):
                act.wait_ge(o_done, t + 1)
                step.then(act.activation(xn[:, t, 512:1024], xn[:, t, 0:512], ACT.Square, accum_out=ss[:, t:t + 1]))
                act.activation(rms[:, t:t + 1], ss[:, t:t + 1], ACT.Sqrt, bias=eps, scale=1.0 / 512).then_inc(o_rooted, 1)
            gelu(2)
            gelu(3)
            table(ACT.Sigmoid)
            for e in range(UT):
                act.wait_ge(glu_ps, e + 1)
                act.activation(sig[:, e, :], yb[e][:, 0:S], ACT.Sigmoid, bias=lc[:, B_GLU + e:B_GLU + e + 1]).then_inc(sig_done, 1)
            split2(19)
            table(ACT.Sqrt)
            for e in range(UT):
                act.wait_ge(glu_done, e + 1)
                act.activation(sq2[:, e, :], sig[:, e, :], ACT.Square).then_inc(sq2_done, 1)
            split2(20)
            act.wait_ge(ssm_ss, 1)
            act.activation(rmsT[:, :], yb[2][:, 0:S], ACT.Sqrt, bias=eps, scale=1.0 / 512).then_inc(ssm_rooted, 1)
            for m in (21, 22, 23):
                split2(m)

            def post_norm(n, k, banks):
                for t in range(TT):
                    a, b = ss[:, 2 * t:2 * t + 1], ss[:, 2 * t + 1:2 * t + 2]
                    act.wait_ge(y_ps, 4 * k + 2 * t + 1)
                    act.activation(xn[:, t, half(0)], banks[2 * t][:, :], ACT.Square, accum_out=a).then_inc(post_sq, 1)
                    act.wait_ge(post_sq, 4 * n + 2 * t + 1)
                    step.did(act.activation(a, a, ACT.Identity, bias=eps, scale=1.0 / D))
                    act.wait_ge(y_ps, 4 * k + 2 * t + 2)
                    act.activation(xn[:, t, half(1)], banks[2 * t + 1][:, :], ACT.Square, accum_out=b).then_inc(post_sq, 1)
                    act.wait_ge(post_sq, 4 * n + 2 * t + 2)
                    step.settle()
                    act.activation(rms[:, t:t + 1], b, ACT.Sqrt, bias=a, scale=1.0 / D).then_inc(post_rooted, 1)

            post_norm(0, NORMS, zb)
            norm(NORMS + 2)
            ffn(NFFN - 1, lambda: modulated(NORMS + 1, lc[:, B_FFN:B_FFN + KC]), True)
            table(ACT.Sqrt)
            post_norm(1, NORMS + 1, yb)

        @block.vector
        def _(dve):
            step = Steps(dve, dve_step)

            def turn_into(r, r_cos, angle, tmp):
                pi = 3.1415925
                step.then(dve.tensor_scalar(tmp, angle, 1 / TWO_PI, ROUND, ALU.mult, ALU.add))
                step.then(dve.tensor_scalar(tmp, tmp, -ROUND, None, ALU.add))
                for n, piece in enumerate(split_two_pi(4, 9)):
                    step.then(dve.scalar_tensor_tensor(r, tmp, -piece, r if n else angle, ALU.mult, ALU.add))
                step.then(dve.tensor_scalar(r, r, pi, -pi, ALU.min, ALU.max))
                step.then(dve.tensor_scalar(tmp, r, math.pi / 2, -TWO_PI, ALU.is_gt, ALU.mult))
                step.then(dve.scalar_tensor_tensor(r_cos, r, math.pi / 2, tmp, ALU.add, ALU.add))
                return dve.tensor_scalar(r_cos, r_cos, pi, -pi, ALU.min, ALU.max)

            def modulation(k, l, m):
                dve.wait_ge(lc_loaded, 16 * l + 16)
                dve.wait_ge(mod_ps, k + 1)
                step.then(dve.tensor_tensor(mods[:, :], tb[0][:, 0:16], lc[:, L_ADA + 16 * m:L_ADA + 16 * m + 16], ALU.add))
                dve.scalar_tensor_tensor(gs[:, :], mods[:, KC:2 * KC], 1.0, lc[:, L_NORM + KC * m:L_NORM + KC * m + KC], ALU.add, ALU.mult)\
                   .then_inc(mod_done, 1)
                dve.wait_ge(mod_done, k + 1)

            def norm(k):
                for t in range(TT):
                    dve.wait_ge(rms_ready, 2 * k + t + 1)
                    step.then(dve.reciprocal(rstd[:, t:t + 1], rms[:, t:t + 1]))
                    dve.tensor_scalar(xn[:, t, :], x[:, t, :], rstd[:, t:t + 1], None, ALU.mult).then_inc(xn_ready, 1)

            def modulated(kt, gain, shift=None):
                def whole(j):
                    dve.wait_ge(tr_ready, 4 * kt + j + 1)
                    for c in (2 * j, 2 * j + 1):
                        src = yb[j][:, S * (c % 2):S * (c % 2 + 1)]
                        if shift is None:
                            dve.tensor_scalar(hT[:, c, :], src, gain[:, c:c + 1], None, ALU.mult).then_inc(hT_ready, 1)
                        else:
                            dve.tensor_scalar(hT[:, c, :], src, gain[:, c:c + 1], shift[:, c:c + 1], ALU.mult, ALU.add).then_inc(hT_ready, 1)

                def lo(j):
                    dve.wait_ge(hT_hi_done, 4 * kt + j + 1)
                    pair = slice(2 * j, 2 * j + 2)
                    dve.tensor_tensor(hT_lo[:, pair, :], hT[:, pair, :], hT_hi[:, pair, :].bitcast(F32), ALU.subtract).then_inc(hT_lo_done, 1)

                whole(1)
                lo(0)
                whole(3)
                for j in range(1, 4):
                    lo(j)

            def split(mixer, m, n):
                dve.wait_ge(w_hi_done, SPLITS * mixer + m + 1)
                dve.tensor_tensor(dn_lo[:, (m + 2) % SLOTS, :], ring[:, n % RING, :], dn_hi[:, (m + 2) % SLOTS, :].bitcast(F32), ALU.subtract).then_inc(w_lo_done, 1)

            def split_gu(n, b):
                dve.wait_ge(gu_hi_done, n + 1)
                dve.tensor_tensor(gu_lo[:, b, :, :, :].rearrange("p h c n -> p (h c n)"), raw_gu[:, b, :],
                                  gu_hi[:, b, :, :, :].rearrange("p h c n -> p (h c n)").bitcast(F32), ALU.subtract).then_inc(gu_lo_done, 1)

            def ffn(f, modulate, split_first, in_between=None):
                base = FB * f

                def split_dn(n, b):
                    dve.wait_ge(dn_hi_done, base + n + 1)
                    dve.tensor_tensor(dn_lo[:, b, :], raw_dn[:, b, :], dn_hi[:, b, :].bitcast(F32), ALU.subtract).then_inc(dn_lo_done, 1)

                def hidden(n, b, reused=True):
                    dve.wait_ge(silu_done, base + n + 1)
                    dve.tensor_tensor(prod[:, b, :], sg[:, b, :], gu_bank[b][:, S:2 * S], ALU.mult).then_inc(prod_done, 1)
                    if reused:
                        dve.wait_ge(dn_used, (FB - 1) * f + n - 1)
                    dve.wait_ge(prod_done, base + n + 1)
                    dve.tensor_copy(act_hi[:, b, :], prod[:, b, :]).then_inc(act_hi_done, 1)
                    dve.wait_ge(act_hi_done, base + n + 1)
                    dve.tensor_tensor(act_lo[:, b, :], prod[:, b, :], act_hi[:, b, :].bitcast(F32), ALU.subtract).then_inc(act_done, 1)

                if split_first:
                    split_gu(base, 0)
                modulate()
                split_dn(0, 0)
                split_gu(base + 1, 1)
                for b in range(2):
                    hidden(b, b, reused=False)
                    split_gu(base + b + 2, b)
                    split_dn(b + 1, 1 - b)
                for part_, blocks in enumerate(((1, FB // 4 + 1), (FB // 4 + 1, FB // 2 - 1))):
                    if part_ and in_between:
                        in_between()
                    with dve.Fori(*blocks) as i:
                        for b in range(2):
                            hidden(2 * i + b, b)
                            split_gu(base + 2 * i + b + 2, b)
                            split_dn(2 * i + b + 1, 1 - b)
                hidden(FB - 2, 0)
                split_dn(FB - 1, 1)
                hidden(FB - 1, 1)

            def gate(k):
                dve.wait_ge(gbias_loaded, 16 * k + 16)
                for b in range(2):
                    dve.wait_ge(gate_ps, 2 * k + b + 1)
                    dve.tensor_tensor(gate_b[:, half(b)], gate_b[:, half(b)], tb[b][:, :], ALU.add).then_inc(gate_done, 1)

            def residual(k, scale):
                dve.wait_ge(gate_done, 2 * k + 4)
                for t in range(TT):
                    for b in range(2):
                        dve.wait_ge(y_ps, 4 * k + 2 * t + b + 1)
                        step.did(dve.scalar_tensor_tensor(xn[:, t, half(b)], yb[2 * t + b][:, :], scale, gate_b[:, half(b)], ALU.mult, ALU.mult))
                    step.settle()
                    for b in range(2):
                        dve.tensor_tensor(x[:, t, half(b)], x[:, t, half(b)], xn[:, t, half(b)], ALU.add).then_inc(x_ready, 1)

            def rope(to, straight, swapped, heads, scratch):
                wide = [P, heads, S]
                step.did(dve.tensor_tensor(scratch[:, 0, 0:heads, :], straight, cosT[:, :].unsqueeze(1).to_broadcast(wide), ALU.mult))
                step.then(dve.tensor_tensor(scratch[:, 1, 0:heads, :], swapped, sinT[:, :].unsqueeze(1).to_broadcast(wide), ALU.mult))
                for rows_, dst in to:
                    last = dve.tensor_tensor(dst, scratch[rows_, 0, 0:heads, :], scratch[rows_, 1, 0:heads, :], ALU.add)
                    yield last

            def mixer(l):
                base = TILES * l
                dve.wait_ge(masks_loaded, 16)

                def lo(m):
                    split(l, m, m + (m >= POOL_UNIT))

                def root(a):
                    dve.wait_ge(lat_rooted, 2 * l + a + 1)
                    step.then(dve.reciprocal(lat_rms[:, a, :], lat_rms[:, a, :]))

                def latent(a):
                    first, count, at = ((0, QCH, L_QN), (QCH, KVCH, L_KVN))[a]
                    for c in range(count):
                        step.did(dve.scalar_tensor_tensor(z[:, first + c, :], z[:, first + c, :], lc[:, at + c:at + c + 1], lat_rms[:, a, :],
                                                          ALU.mult, ALU.mult))
                    step.settle()

                def latent_halves(a):
                    which = (slice(0, QCH), slice(QCH, QCH + KVCH))[a]
                    step.then(dve.tensor_copy(lat_hi[:, which, :], z[:, which, :]))
                    dve.tensor_tensor(lat_lo[:, which, :], z[:, which, :], lat_hi[:, which, :].bitcast(F32), ALU.subtract).then_inc(lat_done, 1)

                def rope_key():
                    dve.wait_ge(tile_out, base + ZT)
                    step.did(dve.memset(krz[64:128, 0, :], 0.0))
                    step.did(dve.memset(krz[0:64, 1, :], 0.0))
                    for last in rope([(slice(0, 64), krz[0:64, 0:1, :]), (slice(64, 128), krz[64:128, 1:2, :])], z[:, 5:6, :], z[:, 6:7, :], 1, rot):
                        last.then_inc(kr_ready, 1)

                end = PADT + S
                sums = (sumA[:, 0], sumB[:, 0], sumA[:, 2], sumB[:, 2])

                def pool_sums():
                    step.did(dve.memset(upad[:, :, 0:PADT], 0.0))
                    dve.wait_ge(tile_out, base + 9)
                    step.settle()
                    step.then(dve.tensor_tensor(sumA[:, :, 1:end], upad[:, :, 1:end], upad[:, :, 0:end - 1], ALU.add))

                def more_sums():
                    step.then(dve.tensor_tensor(sumB[:, :, 3:end], sumA[:, 1:4, 3:end], sumA[:, 1:4, 1:end - 2], ALU.add))
                    step.then(dve.tensor_tensor(sumA[:, 2:4, 7:end], sumB[:, 1:3, 7:end], sumB[:, 1:3, 3:end - 4], ALU.add))
                    step.then(dve.tensor_tensor(sumB[:, 2, 15:end], sumA[:, 3, 15:end], sumA[:, 3, 7:end - 8], ALU.add))

                def pool_diffs():
                    for g, s in enumerate(sums):
                        ratio = cst[:, C_RATIO + PADT * g:C_RATIO + PADT * (g + 1)]
                        step.did(dve.tensor_tensor(s[:, PADT:2 * PADT], s[:, PADT:2 * PADT], ratio, ALU.mult))
                    step.settle()
                    for g, s in enumerate(sums):
                        dve.scalar_tensor_tensor(s[:, PADT:end], s[:, PADT:end], 0.5 ** (g + 1), upad[:, g, PADT:end], ALU.mult, ALU.subtract)\
                           .then_inc(diff_ready, 1)

                def rope_queries():
                    dve.wait_ge(tile_out, base + ZT + 8)
                    dve.wait_ge(kr_ready, 2 * l + 2)
                    for last in rope([(slice(0, P), qr[:, :, :])], qrs[:, 0:2, :], qrs[:, 2:4, :], 2, rot):
                        last.then_inc(qr_ready, 1)

                def masked(h):
                    dve.wait_ge(sc_ps, HEADS * l + h + 1)
                    dve.tensor_tensor(pm[:, h, :], zb[(ZT + 18 + h) % 4][:, 0:384], mask, ALU.add).then_inc(sm_done, 1)
                    dve.wait_ge(sm_done, HEADS * l + h + 1)
                    step.did(dve.reduce_max(rmax[:, h, 0:1], pm[:, h, 0:P], axis=AX.X))
                    step.then(dve.reduce_max(rmax[:, h, 1:2], pm[:, h, P:P + S], axis=AX.X))
                    dve.tensor_scalar(negm[:, h, :], rmax[:, h, :], -MLA_SCALE, None, ALU.mult).then_inc(negm_ready, 1)

                def probabilities(h):
                    dve.wait_ge(p_ready, 2 * (HEADS * l + h + 1))
                    step.then(dve.reciprocal(prec[:, h, :], psum_[:, h, :]))
                    for t, part_ in enumerate((slice(0, P), slice(P, P + S))):
                        dve.tensor_scalar(pm[:, h, part_], pm[:, h, part_], prec[:, h, t:t + 1], None, ALU.mult).then_inc(pn_ready, 1)

                def mixed(c):
                    dve.wait_ge(tile_out, base + (ZT + 8 + HEADS + c + 1 if c < POOLG else TILES - (5, 3, 1, 0)[c - POOLG]))
                    dve.tensor_tensor(hT_lo[:, c, :], hT[:, c, :], hT_hi[:, c, :].bitcast(F32), ALU.subtract).then_inc(mix_done, 1)

                for m in range(2, 6):
                    lo(m)
                root(0)
                latent(0)
                lo(6)
                latent_halves(0)
                lo(7)
                root(1)
                latent(1)
                lo(8)
                latent_halves(1)
                lo(9)
                lo(10)
                pool_sums()
                lo(11)
                lo(12)
                more_sums()
                lo(13)
                rope_key()
                pool_diffs()
                lo(14)
                rope_queries()
                lo(15)
                for c in range(POOLG):
                    mixed(c)
                masked(0)
                lo(16)
                masked(1)
                lo(17)
                masked(2)
                masked(3)
                lo(18)
                for h in range(HEADS):
                    probabilities(h)
                lo(19)
                lo(20)
                lo(21)
                lo(22)
                for c in range(POOLG, KC):
                    mixed(c)
                lo(23)

            dve.wait_ge(cst_loaded, 16)
            a_re, a_im = cst[:, C_ARE:C_ARE + ST], cst[:, C_AIM:C_AIM + ST]
            dve.wait_ge(prep_act, 1)
            step.did(dve.tensor_tensor(sp[:, 1, :], a_re, sp[:, 0, :], ALU.mult))
            step.then(dve.tensor_tensor(sp[:, 2, :], a_im, sp[:, 0, :], ALU.mult))
            step.did(turn_into(sp[:, 3, :], sp[:, 4, :], sp[:, 2, :], sp[:, 5, :]))
            dve.wait_ge(pos_loaded, 16)
            step.then(dve.tensor_copy(xn[:, 1, S:2 * S], pos_i))
            step.then(dve.tensor_scalar(xn[:, 0, 2 * S:3 * S], xn[:, 1, S:2 * S], cst[:, C_FREQ:C_FREQ + 1], None, ALU.mult))
            turn_into(xn[:, 0, 0:S], xn[:, 0, S:2 * S], xn[:, 0, 2 * S:3 * S], xn[:, 1, 2 * S:3 * S]).then_inc(prep_args, 1)

            def coefficients():
                dve.wait_ge(prep_act, 6)
                nr, li, den = sp[:, 0, :], sp[:, 1, :], sp[:, 2, :]
                step.did(dve.tensor_tensor(nr, mag[:, :], cos1[:, :], ALU.mult))
                step.did(dve.tensor_tensor(li, mag[:, :], sin1[:, :], ALU.mult))
                step.did(dve.tensor_tensor(den, a_re, a_re, ALU.mult))
                step.did(dve.tensor_tensor(sp[:, 3, :], a_im, a_im, ALU.mult))
                step.then(dve.tensor_scalar(sinT[:, :], sinT[:, :], cst[:, C_SIGN:C_SIGN + 1], None, ALU.mult))
                step.did(dve.tensor_scalar(nr, nr, -1.0, None, ALU.add))
                step.then(dve.tensor_tensor(den, den, sp[:, 3, :], ALU.add))
                step.did(dve.reciprocal(den, den))
                step.did(dve.tensor_tensor(sp[:, 3, :], nr, a_re, ALU.mult))
                step.did(dve.tensor_tensor(sp[:, 4, :], li, a_im, ALU.mult))
                step.did(dve.tensor_tensor(sp[:, 5, :], li, a_re, ALU.mult))
                step.then(dve.tensor_tensor(sp[:, 6, :], nr, a_im, ALU.mult))
                step.did(dve.tensor_tensor(sp[:, 3, :], sp[:, 3, :], sp[:, 4, :], ALU.add))
                step.then(dve.tensor_tensor(sp[:, 5, :], sp[:, 5, :], sp[:, 6, :], ALU.subtract))
                step.did(dve.tensor_tensor(cre[:, :], sp[:, 3, :], den, ALU.mult))
                dve.tensor_tensor(cim[:, :], sp[:, 5, :], den, ALU.mult).then_inc(prep_dve, 1)

            dve.wait_ge(c_ready, 1)
            dve.wait_ge(ones_set, 3)

            def chunk_sums(n):
                dve.wait_ge(pro_loaded[n], 16)
                at = [0, 0]
                for c in range(KC):
                    for i in range(2):
                        to, w = pro_sums(n)[:, tok(i)], pro_slot(n)[:, c, tok(i)]
                        if c == 0:
                            last = dve.tensor_scalar(to, w, c_act[:, 0:1], None, ALU.mult)
                        else:
                            dve.wait_ge(dve_step, at[i])
                            last = dve.scalar_tensor_tensor(to, w, c_act[:, c:c + 1], to, ALU.mult, ALU.add)
                        if c < KC - 1:
                            step.did(last)
                        else:
                            last.then_inc(pro_done, 1)
                        at[i] = step.n

            rows_done = 0
            for n in (DVE_CHUNKS[0], 0, 2, 3, DVE_CHUNKS[1], 5, 6, 7):
                if n in DVE_CHUNKS:
                    chunk_sums(n)
                    continue
                if n == 5:
                    coefficients()
                if n == 7:
                    dve.wait_ge(x_loaded, 16)
                    dve.sem_inc(x_ready, 4)
                rows_done += 1
                dve.wait_ge(pro_rows, rows_done)
                dve.tensor_copy(pro_sums(n)[0:1, :], pro_row(n)).then_inc(pro_done, 1)
            dve.sem_inc(gate_done, 2)

            with dve.Fori(0, DEPTH) as l:
                step.enter_layers(l, DVE_LAYER)
                for m in range(3):
                    k = 3 * l + m
                    norm(k)
                    if m == 1:
                        split(l, 1, 1)
                    modulation(k, l, m)
                    if m == 1:
                        modulated(k, gs, mods)
                        mixer(l)
                        split_gu(FB * (2 * l + 1), 0)
                        gate(k)
                    else:
                        ffn(2 * l + m // 2, lambda: modulated(k, gs, mods), m == 0, lambda: gate(k))
                        if m == 0:
                            split(l, 0, 0)
                    residual(k, 1.0 if m == 1 else 0.5)
                step.leave_layers()

            dve.wait_ge(final_loaded, 16)
            for t in range(TT):
                dve.wait_ge(rms_ready, 2 * NORMS + t + 1)
                step.then(dve.reciprocal(rstd[:, t:t + 1], rms[:, t:t + 1]))
                dve.scalar_tensor_tensor(x[:, t, :], x[:, t, :], rstd[:, t:t + 1], row_b[:, :], ALU.mult, ALU.mult).then_inc(x_ready, 2)

            def skip(u):
                dve.wait_ge(c_ps, 4 * u + 4)
                dve.scalar_tensor_tensor(y2[:, u, :], u2[:, u, :], lc[:, B_SKIP + u:B_SKIP + u + 1], yb[2 + u % 2][:, 0:S],
                                         ALU.mult, ALU.add).then_inc(skip_done, 1)

            def maxima(h):
                dve.wait_ge(sc2_ps, h + 1)
                step.did(dve.reduce_max(rmax2[:, h, 0:1], zb[2 + h % 2][:, 0:P], axis=AX.X))
                step.then(dve.reduce_max(rmax2[:, h, 1:2], zb[2 + h % 2][:, P:P + S], axis=AX.X))
                dve.tensor_scalar(negm2[:, h, :], rmax2[:, h, :], -HD2 ** -0.5, None, ALU.mult).then_inc(negm2_done, 1)

            def lo(m):
                split(DEPTH, m, m)

            dve.wait_ge(lc_loaded, 16 * DEPTH + 16)
            lo(0)
            norm(NORMS + 1)
            lo(1)
            modulated(NORMS, lc[:, B_MIX:B_MIX + KC])
            lo(2)
            lo(3)
            for s in range(ST):
                if s < 14:
                    lo(4 + s)
                dve.wait_ge(bu_ps, s + 1)
                bu = yb[s % 2][:, :].rearrange("p (r n) -> p r n", r=2)
                for to, table in ((ma, ecos), (mb, esin)):
                    dve.tensor_tensor(to[:, :, :], bu, table[:, s, :].unsqueeze(1).to_broadcast([P, 2, S]), ALU.mult).then_inc(bu_used, 1)
                dve.wait_ge(bu_used, 2 * s + 2)
                step.did(dve.tensor_tensor(vin[:, 0, :], ma[:, 0, :], mb[:, 1, :], ALU.add))
                step.then(dve.tensor_tensor(vin[:, 1, :], ma[:, 1, :], mb[:, 0, :], ALU.subtract))
                if s >= 3:
                    dve.wait_ge(turned, 2 * (s - 2))
                for r in range(2):
                    last = dve.tensor_tensor_scan(ysc[:, s % 3, r, :], mag[:, s:s + 1].to_broadcast([P, S]), vin[:, r, :], 0.0, ALU.mult, ALU.add)
                    if r == 0:
                        step.did(last)
                last.then_inc(scanned, 1)
                if s % 4 == 1 and s > 4:
                    skip(s // 4 - 1)
                if s in (10, 12, 14, 15):
                    h = 2 * (10, 12, 14, 15).index(s)
                    maxima(h)
                    maxima(h + 1)
            dve.wait_ge(p2_done, 2 * HEADS2)
            step.then(dve.reciprocal(prec2[:, :, :], psum2[:, :, :]))
            dve.wait_ge(o_ps, HEADS2)
            for t in range(TT):
                dve.tensor_tensor(xn[:, t, 0:512].rearrange("p (h n) -> p h n", n=HD2), zb[t][:, :].rearrange("p (h n) -> p h n", n=HD2),
                                  prec2[:, t, :].unsqueeze(2).to_broadcast([P, HEADS2, HD2]), ALU.mult).then_inc(o_done, 1)
            for t in range(TT):
                dve.wait_ge(o_rooted, t + 1)
                step.then(dve.reciprocal(rstd[:, t:t + 1], rms[:, t:t + 1]))
                dve.tensor_scalar(xn[:, t, 512:1024], xn[:, t, 0:512], rstd[:, t:t + 1], None, ALU.mult).then_inc(on_done, 1)
            lo(18)
            skip(UT - 1)

            def mix_halves(c):
                pair = slice(c, c + 2)
                step.then(dve.tensor_copy(hT_hi[:, pair, :], hT[:, pair, :]))
                dve.tensor_tensor(hT_lo[:, pair, :], hT[:, pair, :], hT_hi[:, pair, :].bitcast(F32), ALU.subtract).then_inc(mix2_done, 1)

            for j in range(2):
                dve.wait_ge(ot_ps, j + 1)
                for c in (2 * j, 2 * j + 1):
                    step.did(dve.tensor_scalar(hT[:, UT + c, :], tb[j][:, S * (c % 2):S * (c % 2 + 1)], lc[:, B_ATT + c:B_ATT + c + 1], None, ALU.mult))
                step.settle()
                mix_halves(UT + 2 * j)
            for e in range(UT):
                dve.wait_ge(sig_done, e + 1)
                dve.tensor_tensor(sig[:, e, :], sig[:, e, :], y2[:, e, :], ALU.mult).then_inc(glu_done, 1)
            lo(19)
            lo(20)
            dve.wait_ge(ssm_rooted, 1)
            step.then(dve.reciprocal(rstdT[:, :], rmsT[:, :]))
            for j in range(2):
                for c in (2 * j, 2 * j + 1):
                    step.did(dve.scalar_tensor_tensor(hT[:, c, :], sig[:, c, :], lc[:, B_SSM + c:B_SSM + c + 1], rstdT[:, :], ALU.mult, ALU.mult))
                step.settle()
                mix_halves(2 * j)
            for m in (21, 22, 23):
                lo(m)

            def post_norm(n, row, banks):
                for t in range(TT):
                    for b in range(2):
                        dve.wait_ge(post_sq, 4 * n + 2 * t + b + 1)
                        step.did(dve.tensor_tensor(xn[:, t, half(b)], banks[2 * t + b][:, :], row[:, half(b)], ALU.mult))
                    dve.wait_ge(post_rooted, 2 * n + t + 1)
                    step.then(dve.reciprocal(rstd[:, t:t + 1], rms[:, t:t + 1]))
                    for b in range(2):
                        dve.scalar_tensor_tensor(x[:, t, half(b)], xn[:, t, half(b)], rstd[:, t:t + 1], x[:, t, half(b)], ALU.mult, ALU.add)\
                           .then_inc(x_ready, 1)

            dve.wait_ge(row_loaded, 16)
            post_norm(0, row_b, zb)
            norm(NORMS + 2)
            ffn(NFFN - 1, lambda: modulated(3 * DEPTH + 1, lc[:, B_FFN:B_FFN + KC]), True)
            dve.wait_ge(gbias_loaded, 16 * 3 * DEPTH + 16)
            post_norm(1, gate_b, yb)


def tiles_of(w):
    return w.reshape(KC, P, -1, P).transpose(2, 1, 0, 3)


def columns(v):
    return np.asarray(v).reshape(-1, P).T


def kernel(**inputs):
    import concourse.bacc as bacc
    from concourse.bass_utils import run_bass_kernel_spmd

    a = {k: np.asarray(v) for k, v in inputs.items()}
    f32 = np.float32

    def ffn_weights(kind):
        first = [a[f"ffn{n}_w_{kind}"][l] for l in range(DEPTH) for n in (1, 2)]
        return [*first, a[f"w_{kind}_2"][0]]

    gu = np.empty((NFFN, FB, P, 2, KC, P), f32)
    dn = np.empty((NFFN, FB, P, D), f32)
    for f, (g, u, d) in enumerate(zip(*map(ffn_weights, ("gate", "up", "down")))):
        gu[f, :, :, 0], gu[f, :, :, 1], dn[f] = tiles_of(g), tiles_of(u), d.reshape(FB, P, D)

    ada = a["ada_w"].reshape(DEPTH, KC, P, 36, S).transpose(0, 3, 2, 1, 4).reshape(DEPTH * 36, P, KC * S)

    kr = np.arange(1152, 1216)
    z_cols = np.concatenate([np.arange(512, 1152), np.arange(512), kr, kr, np.roll(kr, 32), np.roll(kr, 32)])
    q_cols = np.arange(HEADS * 192).reshape(HEADS, 192)
    rope = q_cols[:, 128:]
    q_cols = np.concatenate([q_cols[:, :128].ravel(), rope.ravel(), np.roll(rope, 32, 1).ravel()])
    kv_cols = np.arange(HEADS * 256).reshape(HEADS, 2, P).transpose(1, 0, 2).ravel()
    mix = np.zeros((DEPTH, UNITS, P, D), f32)
    for l in range(DEPTH):
        mix[l, :ZT] = tiles_of(a["w_in"][l][:, z_cols]).reshape(ZT, P, D)
        q = a["w_q_b"][l][:, q_cols].reshape(QCH, P, 8, P).transpose(1, 2, 0, 3).reshape(P, QCH, D)
        mix[l, ZT:ZT + QCH] = q.transpose(1, 0, 2)
        kv = a["w_kv_b"][l][:, kv_cols].reshape(KVCH, P, 2, HEADS, P)
        mix[l, ZT + QCH] = kv[:, :, 0].transpose(1, 2, 0, 3).reshape(P, D)
        mix[l, POOL_UNIT + 1] = kv[:, :, 1].transpose(1, 0, 2, 3).reshape(P, D)
        mix[l, POOL_UNIT, :, :512] = a["pool_w"][l].transpose(1, 0, 2).reshape(P, 512)
        mix[l, UNITS - KC:] = a["w_out"][l].reshape(KC, P, D)
    mix = mix.reshape(DEPTH * UNITS, P, D)
    w_in = a["w_in_2"][0]
    mix2 = np.empty((UNITS2 + 2, P, D), f32)
    mix2[:12] = tiles_of(w_in[:, :1536]).reshape(12, P, D)
    mix2[12:16] = w_in[:, 1536:].reshape(4, 2, P, 512).transpose(0, 2, 1, 3).reshape(4, P, D)
    mix2[16:UNITS2] = np.roll(a["w_out_2"][0].reshape(KC, P, D), UT, 0)
    mix2[UNITS2:] = a["w_glu_2"][0].reshape(2, 2, P, 512).transpose(0, 2, 1, 3).reshape(2, P, D)

    consts = np.zeros((P, C_N), f32)
    consts[:, C_C:C_C + KC] = columns(a["c"][0])
    consts[:, C_FREQ] = np.tile((1.0 / (f32(10000.0) ** (np.arange(0, 64, 2, dtype=f32) / f32(64)))).astype(f32), 4)
    consts[:, C_SIGN] = np.tile(np.repeat([-1.0, 1.0], 32), 2)
    consts[:, C_ARE:C_ARE + ST] = columns(a["ssm_a_re_2"][0])
    consts[:, C_AIM:C_AIM + ST] = columns(a["ssm_a_im_2"][0])
    consts[:, C_DT:C_DT + ST] = columns(np.repeat(a["ssm_log_dt_2"][0], 64))
    for g in range(POOLG):
        w = 2 ** (g + 1)
        consts[:, C_RATIO + PADT * g:C_RATIO + PADT * (g + 1)] = w / np.minimum(np.arange(PADT) + 1, w)
    tri = np.where(np.arange(P)[:, None] >= np.arange(P)[None, :], 0.0, MASKED)
    consts[:, C_MASK:C_MASK + P] = consts[:, C_MASK + S:C_MASK + S + P] = tri
    consts[:, C_ID:C_ID + P] = np.eye(P)
    for at, name, order in ((C_BRE, "ssm_b_re_2", None), (C_BIM, "ssm_b_im_2", None), (C_CRE, "ssm_c_re_2", 1), (C_CIM, "ssm_c_im_2", 1)):
        w = a[name][0].transpose(0, 2, 1) if order else a[name][0]
        consts[:, at:at + 256] = w.reshape(ST, P, 16).transpose(1, 0, 2).reshape(P, 256)

    cols = np.zeros((DEPTH + 1, P, L_N), f32)
    gate_rows = np.empty((3 * DEPTH, D), f32)
    for l in range(DEPTH):
        b = a["ada_b"][l].reshape(3, 3, D)
        for m in range(3):
            cols[l, :, L_ADA + 16 * m:L_ADA + 16 * m + 16] = columns(b[m, :2])
            gate_rows[3 * l + m] = b[m, 2]
        for m, name in enumerate(("ffn1_norm", "mix_norm", "ffn2_norm")):
            cols[l, :, L_NORM + KC * m:L_NORM + KC * (m + 1)] = columns(a[name][l])
        cols[l, :, L_PSC:L_PSC + 4] = columns(a["pool_scale"][l])
        cols[l, :, L_QN:L_QN + QCH] = columns(a["q_a_norm"][l])
        cols[l, :, L_KVN:L_KVN + KVCH] = columns(a["kv_a_norm"][l])
    for at, name in ((B_MIX, "g_pre_mix_2"), (B_FFN, "g_pre_ffn_2"), (B_SSM, "g_ssm_out_2"), (B_ATT, "g_attn_out_2"), (B_GLU, "b_glu_2"), (B_SKIP, "ssm_d_2")):
        got = columns(a[name][0])
        cols[DEPTH, :, at:at + got.shape[1]] = got
    rows = np.stack([a["final_norm"], a["g_post_mix_2"][0], a["g_post_ffn_2"][0]])

    nc = bacc.Bacc("TRN2", target_bir_lowering=False, num_devices=1)
    arrays = {
        "x_in": a["x"][0], "positions": a["positions"], "consts": consts, "cols": cols, "gate_rows": gate_rows, "rows": rows, "ada": ada,
        "ffn_gu": gu.reshape(NFFN * FB, P, 2 * KC * P), "ffn_dn": dn.reshape(NFFN * FB, P, D), "mix_w": mix, "mix2_w": mix2,
    }
    arrays = {k: np.ascontiguousarray(v) for k, v in arrays.items()}
    aps = [nc.dram_tensor(k, v.shape, mybir.dt.from_np(v.dtype), kind="ExternalInput").ap() for k, v in arrays.items()]
    out = nc.dram_tensor("x_out", (S, D), F32, kind="ExternalOutput").ap()
    program(nc, *aps, out)
    r = run_bass_kernel_spmd(nc, [arrays], core_ids=[0])
    return r.results[0]["x_out"].reshape(1, S, D)
```
